# Optimizing a Trainium2 kernel written in Bass

```python
import jax, jax.numpy as jnp
from jax import lax
import numpy as np

D_MODEL = 2048
BATCH = 1
SEQ = 512
DEPTH = 1

N_MIXERS = 4
D_FF = 4 * D_MODEL
EPS = 1e-6
NEG = -1e30
FORCE = 1e30

CONV_WIDTH = 31
NSA_HEADS = 16
NSA_HEAD_DIM = D_MODEL // NSA_HEADS
NSA_KV_GROUPS = 4
NSA_HPG = NSA_HEADS // NSA_KV_GROUPS
CMP_BLOCK = 32
CMP_STRIDE = 16
SEL_BLOCK = 64
SEL_TOPK = 16
WINDOW = 512
NSA_Q_CHUNK = 32
POOL_WINDOWS = (2, 4, 8, 16)
POOL_GROUPS = len(POOL_WINDOWS)
POOL_GROUP_DIM = D_MODEL // POOL_GROUPS
MLA_HEADS = 16
MLA_NOPE_DIM = 128
MLA_ROPE_DIM = 64
MLA_V_DIM = 128
MLA_Q_RANK = 512
MLA_KV_RANK = 256
ROPE_THETA = 10000.0
MLA_Q_CHUNK = 128

N_USES = tuple((DEPTH - m + N_MIXERS - 1) // N_MIXERS for m in range(N_MIXERS))

kernel_name = "hybrid_conv_nsa_pool_mla_trunk"

def rms_norm(x, g):
    xf = x.astype(jnp.float32)
    y = xf * lax.rsqrt(jnp.mean(xf * xf, axis=-1, keepdims=True) + EPS)
    return (y * g.astype(jnp.float32)).astype(x.dtype)

def layer_norm(x, g, b):
    xf = x.astype(jnp.float32)
    mu = jnp.mean(xf, axis=-1, keepdims=True)
    var = jnp.mean(jnp.square(xf - mu), axis=-1, keepdims=True)
    y = (xf - mu) * lax.rsqrt(var + EPS) * g.astype(jnp.float32) + b.astype(jnp.float32)
    return y.astype(x.dtype)

def masked_softmax(s, mask):
    s = jnp.where(mask, s.astype(jnp.float32), NEG)
    m = jnp.max(s, axis=-1, keepdims=True)
    e = jnp.where(mask, jnp.exp(s - m), 0.0)
    return e / jnp.maximum(jnp.sum(e, axis=-1, keepdims=True), 1e-30)

def apply_rope(x, cos, sin):
    x1, x2 = jnp.split(x.astype(jnp.float32), 2, axis=-1)
    return jnp.concatenate([x1 * cos - x2 * sin, x1 * sin + x2 * cos], axis=-1).astype(x.dtype)

def sq_relu_mlp(h, w1, w2):
    return jnp.square(jax.nn.relu(h @ w1)) @ w2

def conformer_conv(h, w_in, b_in, w_dw, b_dw, ln_g, ln_b, w_out, b_out):
    u = h @ w_in + b_in
    a, gt = jnp.split(u, 2, axis=-1)
    u = a * jax.nn.sigmoid(gt)
    u = lax.conv_general_dilated(
        u, w_dw[:, None, :].astype(u.dtype), window_strides=(1,),
        padding=[(CONV_WIDTH - 1, 0)],
        dimension_numbers=('NWC', 'WIO', 'NWC'),
        feature_group_count=D_MODEL) + b_dw
    u = jax.nn.silu(layer_norm(u, ln_g, ln_b))
    return u @ w_out + b_out

def pool_mixer(h, w, b, scale):
    B_, S_, _ = h.shape
    hg = h.astype(jnp.float32).reshape(B_, S_, POOL_GROUPS, POOL_GROUP_DIM)
    c0 = jnp.pad(jnp.cumsum(hg, axis=1), ((0, 0), (1, 0), (0, 0), (0, 0)))
    t = jnp.arange(S_)
    outs = []
    for gi, win in enumerate(POOL_WINDOWS):
        cg = c0[:, :, gi]
        lo = jnp.maximum(t + 1 - win, 0)
        wsum = cg[:, 1:] - cg[:, lo]
        cnt = jnp.minimum(t + 1, win).astype(jnp.float32)
        outs.append(wsum / cnt[None, :, None] - hg[:, :, gi])
    d = jnp.stack(outs, axis=2).astype(h.dtype)
    y = jnp.einsum('bsgc,gcd->bsgd', d, w).reshape(B_, S_, D_MODEL) + b
    return y * scale

def nsa(h, w_q, w_kv_cmp, w_kv_slc, w_kv_win, cmp_pe, cmp_w1, cmp_w2, w_gate, b_gate, w_o):
    B_, S_, _ = h.shape
    G, HG, DH, QC = NSA_KV_GROUPS, NSA_HPG, NSA_HEAD_DIM, NSA_Q_CHUNK
    q = (h @ w_q).reshape(B_, S_, G, HG, DH)

    def kv(w):
        u = (h @ w).reshape(B_, S_, 2, G, DH)
        return u[:, :, 0], u[:, :, 1]

    kc, vc = kv(w_kv_cmp)
    ks, vs = kv(w_kv_slc)
    kw, vw = kv(w_kv_win)
    gates = jax.nn.sigmoid(h @ w_gate + b_gate).reshape(B_, S_, G, HG, 3)

    n_sub = S_ // CMP_STRIDE
    n_cmp = n_sub - 1

    def compress(x, pe, w1, w2):
        sub = x.reshape(B_, n_sub, CMP_STRIDE, G, DH)
        blk = jnp.concatenate([sub[:, :-1], sub[:, 1:]], axis=2)
        hid = jax.nn.silu(jnp.einsum('bjpgc,pcd->bjgd', blk + pe[:, None, :], w1))
        return hid @ w2

    k_cmp = compress(kc, cmp_pe[0], cmp_w1[0], cmp_w2[0])
    v_cmp = compress(vc, cmp_pe[1], cmp_w1[1], cmp_w2[1])
    cmp_end = jnp.arange(n_cmp) * CMP_STRIDE + CMP_BLOCK - 1

    n_sel = S_ // SEL_BLOCK
    ks_blk = jnp.moveaxis(ks.reshape(B_, n_sel, SEL_BLOCK, G, DH), 3, 1)
    vs_blk = jnp.moveaxis(vs.reshape(B_, n_sel, SEL_BLOCK, G, DH), 3, 1)
    n_topk = min(SEL_TOPK, n_sel)
    sub_per_sel = SEL_BLOCK // CMP_STRIDE
    blk_id = jnp.arange(n_sel)
    bi = jnp.arange(B_)[:, None, None, None]
    gi = jnp.arange(G)[None, :, None, None]

    kw_pad = jnp.pad(kw, ((0, 0), (WINDOW, 0), (0, 0), (0, 0)))
    vw_pad = jnp.pad(vw, ((0, 0), (WINDOW, 0), (0, 0), (0, 0)))
    scale = DH ** -0.5

    def chunk(s0):
        t = s0 + jnp.arange(QC)
        qb = lax.dynamic_slice_in_dim(q, s0, QC, axis=1)
        sc = jnp.einsum('bqghd,bjgd->bghqj', qb, k_cmp) * scale
        p_cmp = masked_softmax(sc, cmp_end[None, :] <= t[:, None])
        o_cmp = jnp.einsum('bghqj,bjgd->bqghd', p_cmp.astype(v_cmp.dtype), v_cmp)
        pg = jnp.pad(jnp.sum(p_cmp, axis=2), ((0, 0), (0, 0), (0, 0), (0, 1)))
        sub_score = pg + jnp.pad(pg[..., :-1], ((0, 0), (0, 0), (0, 0), (1, 0)))
        imp = sub_score.reshape(B_, G, QC, n_sel, sub_per_sel).sum(-1)
        cur = t // SEL_BLOCK
        forced = ((blk_id[None, :] == 0) | (blk_id[None, :] == cur[:, None])
                  | (blk_id[None, :] == cur[:, None] - 1))
        future = blk_id[None, :] > cur[:, None]
        imp = jnp.where(forced, FORCE, jnp.where(future, NEG, imp))
        _, idx = lax.top_k(imp, n_topk)
        ksel = ks_blk[bi, gi, idx]
        vsel = vs_blk[bi, gi, idx]
        kpos = idx[..., None] * SEL_BLOCK + jnp.arange(SEL_BLOCK)
        ss = jnp.einsum('bqghd,bgqnld->bghqnl', qb, ksel) * scale
        smask = (kpos <= t[:, None, None]).reshape(B_, G, 1, QC, -1)
        ps = masked_softmax(ss.reshape(B_, G, HG, QC, -1), smask)
        o_sel = jnp.einsum('bghqm,bgqmd->bqghd', ps.astype(vsel.dtype),
                           vsel.reshape(B_, G, QC, -1, DH))
        kwin = lax.dynamic_slice_in_dim(kw_pad, s0, QC + WINDOW, axis=1)
        vwin = lax.dynamic_slice_in_dim(vw_pad, s0, QC + WINDOW, axis=1)
        wpos = s0 - WINDOW + jnp.arange(QC + WINDOW)
        sw = jnp.einsum('bqghd,bkgd->bghqk', qb, kwin) * scale
        wmask = ((wpos[None, :] <= t[:, None]) & (wpos[None, :] > t[:, None] - WINDOW)
                 & (wpos[None, :] >= 0))
        pw = masked_softmax(sw, wmask)
        o_win = jnp.einsum('bghqk,bkgd->bqghd', pw.astype(vwin.dtype), vwin)
        gb = lax.dynamic_slice_in_dim(gates, s0, QC, axis=1)
        o = gb[..., 0:1] * o_cmp + gb[..., 1:2] * o_sel + gb[..., 2:3] * o_win
        return o.reshape(B_, QC, G * HG * DH)

    o = lax.map(chunk, jnp.arange(S_ // QC) * QC)
    o = jnp.moveaxis(o, 0, 1).reshape(B_, S_, NSA_HEADS * DH)
    return o @ w_o

def mla(h, w_dq, q_norm_g, w_uq, w_dkv, kv_norm_g, w_uk, w_uv, w_o):
    B_, S_, _ = h.shape
    H, QC = MLA_HEADS, MLA_Q_CHUNK
    pos = jnp.arange(S_, dtype=jnp.float32)
    inv_freq = ROPE_THETA ** (-jnp.arange(0, MLA_ROPE_DIM, 2, dtype=jnp.float32) / MLA_ROPE_DIM)
    ang = pos[:, None] * inv_freq[None, :]
    cos, sin = jnp.cos(ang), jnp.sin(ang)
    cq = rms_norm(h @ w_dq, q_norm_g)
    qf = (cq @ w_uq).reshape(B_, S_, H, MLA_NOPE_DIM + MLA_ROPE_DIM)
    q_nope = qf[..., :MLA_NOPE_DIM]
    q_rope = apply_rope(qf[..., MLA_NOPE_DIM:], cos[:, None, :], sin[:, None, :])
    kv = h @ w_dkv
    ckv = rms_norm(kv[..., :MLA_KV_RANK], kv_norm_g)
    k_rope = apply_rope(kv[..., MLA_KV_RANK:], cos, sin)
    k_nope = (ckv @ w_uk).reshape(B_, S_, H, MLA_NOPE_DIM)
    v = (ckv @ w_uv).reshape(B_, S_, H, MLA_V_DIM)
    scale = (MLA_NOPE_DIM + MLA_ROPE_DIM) ** -0.5
    kpos = jnp.arange(S_)

    def block(s0):
        qn = lax.dynamic_slice_in_dim(q_nope, s0, QC, axis=1)
        qr = lax.dynamic_slice_in_dim(q_rope, s0, QC, axis=1)
        s = (jnp.einsum('bqhd,bkhd->bhqk', qn, k_nope)
             + jnp.einsum('bqhr,bkr->bhqk', qr, k_rope)) * scale
        mask = kpos[None, :] <= (s0 + jnp.arange(QC))[:, None]
        p = masked_softmax(s, mask).astype(v.dtype)
        return jnp.einsum('bhqk,bkhd->bqhd', p, v)

    o = lax.map(block, jnp.arange(S_ // QC) * QC)
    o = jnp.moveaxis(o, 0, 1).reshape(B_, S_, H * MLA_V_DIM)
    return o @ w_o

def setup_inputs(seed: int = 0) -> dict:
    key = jax.random.key(seed)
    it = iter(jax.random.split(key, 48))
    f32 = jnp.float32
    NA, NB, NC, ND = N_USES
    D, H, DH, G = D_MODEL, NSA_HEADS, NSA_HEAD_DIM, NSA_KV_GROUPS

    def w(shape, fan_in, gain=1.0):
        return jax.random.normal(next(it), shape, f32) * (gain * fan_in ** -0.5)

    def small(shape, s=0.02):
        return jax.random.normal(next(it), shape, f32) * s

    def gain(shape):
        return 1.0 + jax.random.normal(next(it), shape, f32) * 0.05

    return {
        "x": jax.random.normal(next(it), (BATCH, SEQ, D), f32),
        "c": jax.random.normal(next(it), (BATCH, D), f32),
        "ada_w": w((DEPTH, D, 6 * D), D, 0.5),
        "ada_b": small((DEPTH, 6 * D)),
        "norm1_g": gain((DEPTH, D)),
        "norm2_g": gain((DEPTH, D)),
        "mlp_w1": w((DEPTH, D, D_FF), D),
        "mlp_w2": w((DEPTH, D_FF, D), D_FF),
        "final_g": gain((D,)),
        "conv_w_in": w((NA, D, 2 * D), D),
        "conv_b_in": small((NA, 2 * D)),
        "conv_w_dw": w((NA, CONV_WIDTH, D), CONV_WIDTH),
        "conv_b_dw": small((NA, D)),
        "conv_ln_g": gain((NA, D)),
        "conv_ln_b": small((NA, D)),
        "conv_w_out": w((NA, D, D), D),
        "conv_b_out": small((NA, D)),
        "nsa_w_q": w((NB, D, H * DH), D),
        "nsa_w_kv_cmp": w((NB, D, 2 * G * DH), D),
        "nsa_w_kv_slc": w((NB, D, 2 * G * DH), D),
        "nsa_w_kv_win": w((NB, D, 2 * G * DH), D),
        "nsa_cmp_pe": small((NB, 2, CMP_BLOCK, DH), 0.1),
        "nsa_cmp_w1": w((NB, 2, CMP_BLOCK, DH, DH), CMP_BLOCK * DH),
        "nsa_cmp_w2": w((NB, 2, DH, DH), DH),
        "nsa_w_gate": w((NB, D, 3 * H), D),
        "nsa_b_gate": small((NB, 3 * H)),
        "nsa_w_o": w((NB, H * DH, D), H * DH),
        "pool_w": w((NC, POOL_GROUPS, POOL_GROUP_DIM, POOL_GROUP_DIM), POOL_GROUP_DIM),
        "pool_b": small((NC, D)),
        "pool_scale": 1.0 + small((NC, D), 0.1),
        "mla_w_dq": w((ND, D, MLA_Q_RANK), D),
        "mla_q_norm_g": gain((ND, MLA_Q_RANK)),
        "mla_w_uq": w((ND, MLA_Q_RANK, MLA_HEADS * (MLA_NOPE_DIM + MLA_ROPE_DIM)), MLA_Q_RANK),
        "mla_w_dkv": w((ND, D, MLA_KV_RANK + MLA_ROPE_DIM), D),
        "mla_kv_norm_g": gain((ND, MLA_KV_RANK)),
        "mla_w_uk": w((ND, MLA_KV_RANK, MLA_HEADS * MLA_NOPE_DIM), MLA_KV_RANK),
        "mla_w_uv": w((ND, MLA_KV_RANK, MLA_HEADS * MLA_V_DIM), MLA_KV_RANK),
        "mla_w_o": w((ND, MLA_HEADS * MLA_V_DIM, D), MLA_HEADS * MLA_V_DIM),
    }

def reference(x, c, ada_w, ada_b, norm1_g, norm2_g, mlp_w1, mlp_w2, final_g,
              conv_w_in, conv_b_in, conv_w_dw, conv_b_dw, conv_ln_g, conv_ln_b, conv_w_out, conv_b_out,
              nsa_w_q, nsa_w_kv_cmp, nsa_w_kv_slc, nsa_w_kv_win, nsa_cmp_pe, nsa_cmp_w1, nsa_cmp_w2,
              nsa_w_gate, nsa_b_gate, nsa_w_o,
              pool_w, pool_b, pool_scale,
              mla_w_dq, mla_q_norm_g, mla_w_uq, mla_w_dkv, mla_kv_norm_g, mla_w_uk, mla_w_uv, mla_w_o):
    cs = jax.nn.silu(c)
    for i in range(DEPTH):
        kind, u = i % N_MIXERS, i // N_MIXERS
        mod = cs @ ada_w[i] + ada_b[i]
        sh1, sc1, g1, sh2, sc2, g2 = [m[:, None, :] for m in jnp.split(mod, 6, axis=-1)]
        h = rms_norm(x, norm1_g[i]) * (1 + sc1) + sh1
        if kind == 0:
            y = conformer_conv(h, conv_w_in[u], conv_b_in[u], conv_w_dw[u], conv_b_dw[u],
                               conv_ln_g[u], conv_ln_b[u], conv_w_out[u], conv_b_out[u])
        elif kind == 1:
            y = nsa(h, nsa_w_q[u], nsa_w_kv_cmp[u], nsa_w_kv_slc[u], nsa_w_kv_win[u],
                    nsa_cmp_pe[u], nsa_cmp_w1[u], nsa_cmp_w2[u], nsa_w_gate[u], nsa_b_gate[u], nsa_w_o[u])
        elif kind == 2:
            y = pool_mixer(h, pool_w[u], pool_b[u], pool_scale[u])
        else:
            y = mla(h, mla_w_dq[u], mla_q_norm_g[u], mla_w_uq[u], mla_w_dkv[u], mla_kv_norm_g[u],
                    mla_w_uk[u], mla_w_uv[u], mla_w_o[u])
        x = x + g1 * y
        h = rms_norm(x, norm2_g[i]) * (1 + sc2) + sh2
        x = x + g2 * sq_relu_mlp(h, mlp_w1[i], mlp_w2[i])
    return rms_norm(x, final_g)


_drawn_inputs = setup_inputs


def setup_inputs(seed=0):
    import zlib

    import numpy as np

    out = dict(_drawn_inputs(seed))
    spreads = {}
    factors = {'norm1_g': 5.772,
     'conv_b_in': 8.0,
     'conv_b_dw': 8.0,
     'conv_ln_g': 5.117,
     'conv_ln_b': 8.0,
     'conv_b_out': 8.0,
     'norm2_g': 3.304}
    for name, (base, spread) in spreads.items():
        noise = np.random.default_rng([zlib.crc32(name.encode()), seed]).standard_normal(out[name].shape)
        drawn = base * np.exp(spread * noise) if base else spread * noise
        out[name] = __import__('jax').numpy.asarray(drawn.astype(out[name].dtype))
    for name, factor in factors.items():
        out[name] = (out[name] * factor).astype(out[name].dtype)
    return out
```

```python
from contextlib import ExitStack

import numpy as np

import concourse.bass as bass
from concourse import mybir

F32 = mybir.dt.float32
F32R = mybir.dt.float32r
ALU = mybir.AluOpType
ACT = mybir.ActivationFunctionType
ET = mybir.EngineType

P = 128
D = 2048
T = 512
KC = D // P
FF = 4 * D
BLK = 8
NBLK = FF // P // BLK
TAPS = 31
EPS = 1e-6
TILES = 16
U = TILES * P
RAW = 4
WS = 2

A0, A1, B0, B1, C0, W2_0 = 0, 8, 32, 40, 48, 56
NUNITS = C0 + 2 * BLK * NBLK
LO_POOL = B0 + 2

M_G1, M_SC2, M_SH2, M_G2 = 2 * KC, 3 * KC, 4 * KC, 5 * KC
ADA = 6 * KC
ADA_A1, ADA_B0, ADA_B1, ADA_C0 = 24, 12, 16, 12

SMALL_G1 = 2 * KC + 4

PARAMS = [("ada_b", ADA), ("norm1_g", KC), ("norm2_g", KC), ("final_g", KC), ("b_in", 2 * KC), ("b_dw", KC),
          ("ln_g", KC), ("ln_b", KC), ("b_out", KC), ("w_dw", KC * TAPS)]
COL, _n = {}, 0
for _name, _w in PARAMS:
    COL[_name] = _n
    _n += _w
NPAR = _n


def trunk_kernel(nc, xT, c, w, ada, par, out):
    x_d = xT.rearrange("(k p) t -> p k t", p=P)
    out_d = out.rearrange("(k p) t -> p k t", p=P)

    with ExitStack() as ctx:
        def sb(name, shape, dt=F32, scope=ctx):
            return scope.enter_context(nc.sbuf_tensor(name, shape, dt))

        def sem(name):
            return ctx.enter_context(nc.semaphore(name))

        xb = sb("xb", [P, KC * T])
        hhi = sb("hhi", [P, KC * T], F32R)
        hlo = sb("hlo", [P, KC * T], F32R)
        raw = sb("raw", [P, RAW, U])
        whi = sb("whi", [P, WS, U], F32R)
        wlo = sb("wlo", [P, WS, U], F32R)
        pr = sb("pr", [P, NPAR])
        mod = sb("mod", [P, ADA])
        modb = sb("modb", [P, ADA])
        b1p = sb("b1p", [P, 2 * KC])
        g1b = sb("g1b", [P, KC])
        rstd = sb("rstd", [P, T])
        ta = sb("ta", [P, T])
        tb = sb("tb", [P, T])
        sq = sb("sq", [P, T])
        ssum = sb("ssum", [P, T])
        ones = sb("ones", [P, P])
        with ExitStack() as early:
            csb = sb("csb", [P, D], scope=early)
            adar = sb("adar", [P, 2, D], scope=early)
            sig = sb("sig", [P, T], scope=early)
            acc1 = sb("acc1", [P, T], scope=early)
            s1 = sb("s1", [P, T], scope=early)
            s2 = sb("s2", [P, T], scope=early)
        dhi = sb("dhi", [P, BLK * T], F32R)
        dlo = sb("dlo", [P, BLK * T], F32R)
        ps = ctx.enter_context(nc.psum_tensor("ps", [P, 8, T], F32))
        mu = ssum

        def f(ap):
            return ap.bitcast(F32)

        def ch(buf, k, lo=0, n=T):
            return buf[:, bass.ds(k * T + lo, n)]

        def col(name, k, n=1):
            return pr[:, bass.ds(COL[name] + k, n)]

        x_in = [sem(f"x_in{i}") for i in range(4)]
        xr_in = [sem(f"xr_in{i}") for i in range(4)]
        c_in, par_in = sem("c_in"), sem("par_in")
        raw_in = [sem(f"raw_in{i}") for i in range(RAW)]
        ada_in = [sem(f"ada_in{i}") for i in range(2)]
        out_done = sem("out_done")
        ones_set = sem("ones_set")
        cs_ready = sem("cs_ready")
        whi_done = sem("whi_done")
        wlo_done = sem("wlo_done")
        unit_done = sem("unit_done")
        ada_mul = sem("ada_mul")
        ada_used = sem("ada_used")
        small = sem("small")
        xsq_done = sem("xsq_done")
        xsq_used = sem("xsq_used")
        stat_done = sem("stat_done")
        var_done = sem("var_done")
        rstd_done = sem("rstd_done")
        dv = sem("dv")
        ac = sem("ac")
        hf_ready = sem("hf_ready")
        hhi_done = sem("hhi_done")
        hlo_done = sem("hlo_done")
        sig_done = sem("sig_done")
        glu_done = sem("glu_done")
        conv_done = sem("conv_done")
        csq_done = sem("csq_done")
        s1_done = sem("s1_done")
        s2_done = sem("s2_done")
        yg_done = sem("yg_done")
        x1_done = sem("x1_done")
        x1sq_done = sem("x1sq_done")
        ss1_done = sem("ss1_done")
        relu_done = sem("relu_done")
        dsq_done = sem("dsq_done")
        dhi_done = sem("dhi_done")
        dlo_done = sem("dlo_done")
        x2_done = sem("x2_done")
        x2sq_done = sem("x2sq_done")
        ss2_done = sem("ss2_done")
        fin_done = sem("fin_done")

        block = ctx.enter_context(nc.Block())

        def loop(eng, n0, n1):
            return nc.Fori(n0, n1, engines=(eng,))

        def wait_raw(eng, q, off=0):
            eng.wait_ge(raw_in[q % RAW], 16 * (q // RAW + 1) + (16 // RAW) * off)

        def wait_ada(eng, a, off=0):
            eng.wait_ge(ada_in[a % 2], 16 * (a // 2 + 1) + 8 * off)

        @block.sync
        def _(sp):
            sp.dma_start(csb[:], c.partition_broadcast(P)).then_inc(c_in, 16)
            sp.dma_start(pr[:], par).then_inc(par_in, 16)
            for i in range(4):
                sp.dma_start(xb[:, 4 * i * T:4 * (i + 1) * T].rearrange("p (k t) -> p k t", t=T),
                             x_d[:, 4 * i:4 * i + 4, :]).then_inc(x_in[i], 16)

            def load_unit(q, off=0):
                if q >= RAW:
                    sp.wait_ge(wlo_done, q - RAW + 1 + off)
                sp.dma_start(raw[:, q % RAW:q % RAW + 1, :], w[:, bass.ds(q + off, 1), :]
                             ).then_inc(raw_in[q % RAW], 16)

            def load_ada(a, off=0):
                if a >= 2:
                    sp.wait_ge(ada_used, a - 1 + off)
                sp.dma_start(adar[:, a % 2:a % 2 + 1, :], ada[:, bass.ds(a + off, 1), :]
                             ).then_inc(ada_in[a % 2], 16)

            a = 0
            for q in range(A0, A1):
                for _ in range(4):
                    load_ada(a)
                    a += 1
                load_unit(q)
            load_unit(A1)
            load_unit(A1 + 1)
            with loop(ET.SP, 0, 6) as i:
                for s in (0, 2):
                    load_unit(A1 + 2 + s, 4 * i)
                    load_unit(A1 + 3 + s, 4 * i)
                    load_ada(2 * KC + s, 4 * i)
                    load_ada(2 * KC + s + 1, 4 * i)
            a += ADA_A1
            for j in range(8):
                load_unit(B0 + 2 + j)
                for _ in range(3 if j % 2 else 0):
                    load_ada(a)
                    a += 1
                if j % 2 == 0 and j:
                    g = j // 2 - 1
                    sp.wait_ge(hf_ready, KC + 4 * g + 4)
                    sp.dma_start(xb[:, 4 * g * T:4 * (g + 1) * T].rearrange("p (k t) -> p k t", t=T),
                                 x_d[:, 4 * g:4 * g + 4, :]).then_inc(xr_in[g], 16)
            g = 3
            sp.wait_ge(hf_ready, KC + 4 * g + 4)
            sp.dma_start(xb[:, 4 * g * T:4 * (g + 1) * T].rearrange("p (k t) -> p k t", t=T),
                         x_d[:, 4 * g:4 * g + 4, :]).then_inc(xr_in[g], 16)
            for j in range(8):
                load_unit(B1 + 2 + j)
                for _ in range(2):
                    load_ada(a)
                    a += 1
            for j in range(8):
                load_unit(C0 + 2 + j)
                for _ in range(2 if j < 6 else 0):
                    load_ada(a)
                    a += 1
            assert a == ADA
            load_unit(W2_0 + 2)
            load_unit(W2_0 + 3)
            with loop(ET.SP, 1, (NUNITS - W2_0) // RAW) as i:
                for q in range(RAW):
                    load_unit(W2_0 + q, 4 * i)
            for n in range(0, KC, 2):
                sp.wait_ge(fin_done, n + 2)
                sp.dma_start(out_d[:, n:n + 2, :], xb[:, n * T:(n + 2) * T].rearrange("p (k t) -> p k t", t=T)
                             ).then_inc(out_done, 16)
            sp.wait_ge(out_done, 16 * (KC // 2))

        @block.tensor
        def _(pe):
            def product(bank, slot, tile, xhi, xlo, first, last):
                t = slice(tile * P, (tile + 1) * P)
                out = ps[:, bank, :]
                pe.matmul(out, whi[:, slot, t], xhi, start=first, stop=False, skip_group_check=True)
                pe.matmul(out, whi[:, slot, t], xlo, start=False, stop=False, skip_group_check=True)
                return pe.matmul(out, wlo[:, slot, t], xhi, start=False, stop=last, skip_group_check=True)

            def outer_unit(q, s, h0, i=None):
                i, first = (0, s == 0) if i is None else (i, False)
                pe.wait_ge(wlo_done, 2 * i + (q + s + 1))
                for kk in range(2):
                    k = 4 * i + (2 * s + kk)
                    pe.wait_ge(hlo_done, k + (h0 + 1))
                    for o in range(8):
                        last = product(o, s, 8 * kk + o, ch(hhi, k), ch(hlo, k), first and kk == 0, False)
                last.then_inc(unit_done, 1)

            def outer_units(q, h0):
                for s in range(2):
                    outer_unit(q, s, h0)
                with loop(ET.PE, 1, 4) as i:
                    for s in range(2):
                        outer_unit(q, s, h0, i)

            def inner_unit(slot, bank, seen):
                pe.wait_ge(wlo_done, seen)
                for k in range(KC):
                    last = product(bank, slot, k, ch(hhi, k), ch(hlo, k), k == 0, k == KC - 1)
                last.then_inc(unit_done, 1)

            pe.wait_ge(ones_set, 1)
            for k in range(KC):
                pe.wait_ge(xsq_done, k + 1)
                s = pe.matmul(ps[:, 7, :], ones[:], (sq if k % 2 else sig)[:], start=k == 0, stop=k == KC - 1)
                s.then_inc(xsq_used, 1)
            pe.wait_ge(rstd_done, 1)
            outer_units(A0, 0)
            with loop(ET.PE, 0, 6) as i:
                for s in range(2):
                    pe.wait_ge(glu_done, 2 * i + (3 + s))
                    inner_unit(0, 2 * s, 4 * i + (A1 + 2 * s + 1))
                    inner_unit(1, 2 * s + 1, 4 * i + (A1 + 2 * s + 2))
            pe.wait_ge(s1_done, KC + 1)
            pe.matmul(ps[:, 6, :], ones[:], s1[:], start=True, stop=True).then_inc(stat_done, 1)
            pe.wait_ge(s2_done, KC + 1)
            pe.matmul(ps[:, 7, :], ones[:], s2[:], start=True, stop=True).then_inc(stat_done, 1)
            outer_units(B0, KC)
            for s in range(2):
                pe.wait_ge(yg_done, s + 1)
                inner_unit(s, s, B1 + s + 1)
            with loop(ET.PE, 1, 4) as i:
                for s in range(2):
                    pe.wait_ge(yg_done, 2 * i + (7 + s))
                    inner_unit(s, s, 2 * i + (B1 + s + 1))
            pe.wait_ge(ss1_done, KC)
            pe.matmul(ps[:, 2, :], ones[:], ssum[:], start=True, stop=True).then_inc(stat_done, 1)
            outer_units(C0, 2 * KC)

            def w2_unit(m, seen, wait_hidden=None):
                pe.wait_ge(wlo_done, seen)
                for nn in range(2):
                    for k in range(BLK):
                        if wait_hidden is not None and nn == 0:
                            pe.wait_ge(dlo_done, wait_hidden + (k + 1))
                        last = product(4 + 2 * (m % 2) + nn, m % 2, 8 * nn + k, ch(dhi, k), ch(dlo, k),
                                       k == 0, k == BLK - 1)
                last.then_inc(unit_done, 1)

            def w2_block(b):
                pe.wait_ge(x2_done, 16 * b + 1)
                pe.wait_ge(relu_done, 8 * b + 6)
                w2_unit(0, 16 * b + (W2_0 + 1), 8 * b)
                w2_unit(1, 16 * b + (W2_0 + 2))
                with loop(ET.PE, 1, 4) as i:
                    for s in range(2):
                        pe.wait_ge(x2_done, 16 * b + 4 * i + (2 * s - 1))
                        w2_unit(s, 16 * b + 2 * i + (W2_0 + s + 1))

            with loop(ET.PE, 0, NBLK - 1) as b:
                w2_block(b)
                with loop(ET.PE, 0, 4) as i:
                    for s in range(2):
                        pe.wait_ge(relu_done, 8 * b + 2 * i + (BLK + s - 1))
                        inner_unit(s, s, 16 * b + 2 * i + (W2_0 + BLK + s + 1))
            w2_block(NBLK - 1)
            pe.wait_ge(ss2_done, KC)
            pe.matmul(ps[:, 2, :], ones[:], ssum[:], start=True, stop=True).then_inc(stat_done, 1)

        @block.scalar
        def _(act):
            def split_hi(q, off=0):
                wait_raw(act, q, off)
                if q >= WS:
                    act.wait_ge(unit_done, q - WS + 1 + off)
                act.activation(whi[:, q % WS, :], raw[:, q % RAW, :], ACT.Copy).then_inc(whi_done, 1)

            def root(n):
                act.wait_ge(var_done, n)
                act.activation(rstd[:], ta[:], ACT.Sqrt).then_inc(rstd_done, 1)

            def h_hi(k, n):
                act.wait_ge(hf_ready, n + 1)
                act.activation(ch(hhi, k), tb[:], ACT.Copy).then_inc(hhi_done, 1)

            act.wait_ge(c_in, 16)
            act.activation(csb[:], csb[:], ACT.Silu).then_inc(cs_ready, 1)
            for k in range(KC):
                act.wait_ge(x_in[k // 4], 16)
                if k >= 2:
                    act.wait_ge(xsq_used, k - 1)
                act.activation((sq if k % 2 else sig)[:], ch(xb, k), ACT.Square).then_inc(xsq_done, 1)
            root(1)
            for j in range(8):
                h_hi(2 * j, 2 * j)
                split_hi(j)
                h_hi(2 * j + 1, 2 * j + 1)

            act.wait_ge(par_in, 16)

            def sigmoid(c, bank, n):
                act.wait_ge(glu_done, n)
                act.activation(sig[:], ps[:, bank, :], ACT.Sigmoid, bias=col("b_in", c + KC)).then_inc(sig_done, 1)

            def c_square(c):
                act.wait_ge(conv_done, c + 2)
                act.wait_ge(s2_done, c + 1)
                act.activation(sq[:], ch(xb, c), ACT.Square).then_inc(csq_done, 1)

            split_hi(8)
            act.wait_ge(unit_done, A1)
            for c in range(4):
                sigmoid(c, 2 * c + 1, c)
                if c == 0:
                    split_hi(9)

            def ada_sum(a, off):
                act.wait_ge(ada_mul, a - 2 * KC + 1 + off)
                act.activation(adar[:, a % 2, :], adar[:, a % 2, :], ACT.Copy,
                               accum_out=mod[:, bass.ds(a + off, 1)]).then_inc(ada_used, 1)

            with loop(ET.Activation, 0, 6) as i:
                for s in range(2):
                    split_hi(A1 + 2 + 2 * s, 4 * i)
                    split_hi(A1 + 3 + 2 * s, 4 * i)
                    act.wait_ge(unit_done, 4 * i + (A1 + 2 * s + 2))
                    sigmoid(2 * i + (4 + s), 2 * s + 1, 2 * i + (4 + s))
                    ada_sum(2 * KC + 2 * s, 4 * i)
                    ada_sum(2 * KC + 2 * s + 1, 4 * i)
                    c_square(2 * i + s)
            for c in range(12, KC):
                c_square(c)
            root(2)

            def z(k):
                act.wait_ge(hf_ready, KC + k + 1)
                act.wait_ge(hlo_done, KC + k)
                act.activation(sq[:], tb[:], ACT.Silu, scale=col("ln_g", k), bias=col("ln_b", k)).then_inc(ac, 1)
                act.wait_ge(ac, k + 1)
                act.activation(ch(hhi, k), sq[:], ACT.Copy).then_inc(hhi_done, 1)

            for k in range(4):
                z(k)
            for j in range(7):
                split_hi(B0 + 2 + j)
                for k in (4 + 2 * j, 5 + 2 * j):
                    if k < KC:
                        z(k)

            def gated(n, bank):
                if n:
                    act.wait_ge(x1_done, n)
                act.activation(sig[:], ps[:, bank, :], ACT.Identity, scale=modb[:, M_G1 + n:M_G1 + n + 1],
                               bias=g1b[:, n:n + 1]).then_inc(yg_done, 1)

            def x1_square(n):
                act.wait_ge(x1_done, n + 1)
                if n:
                    act.wait_ge(ss1_done, n)
                act.activation(sq[:], ch(xb, n), ACT.Square).then_inc(x1sq_done, 1)

            act.wait_ge(small, SMALL_G1)
            act.wait_ge(unit_done, B1)
            gated(0, 0)
            gated(1, 1)
            split_hi(B1 + 1)
            for n in range(2, 8):
                gated(n, n)
                x1_square(n - 2)
            x1_square(6)
            for j in range(8):
                n = 8 + j
                act.wait_ge(unit_done, B1 + j + 1)
                gated(n, j % 2)
                split_hi(B1 + j + 2)
                x1_square(n - 1)
            x1_square(15)
            root(3)
            for k in range(4):
                h_hi(k, 2 * KC + k)
            for j in range(7):
                split_hi(C0 + 2 + j)
                for k in (4 + 2 * j, 5 + 2 * j):
                    if k < KC:
                        h_hi(k, 2 * KC + k)

            def hidden(j, bank, off=0):
                n = j + off
                if j:
                    act.wait_ge(dlo_done, n)
                act.activation(ta[:], ps[:, bank, :], ACT.Relu).then_inc(relu_done, 1)
                act.wait_ge(relu_done, n + 1)
                act.activation(sq[:], ta[:], ACT.Square).then_inc(dsq_done, 1)
                act.wait_ge(dsq_done, n + 1)
                act.activation(ch(dhi, j % BLK), sq[:], ACT.Copy).then_inc(dhi_done, 1)

            act.wait_ge(ada_used, ADA)
            act.wait_ge(unit_done, W2_0)
            hidden(0, 0)
            split_hi(W2_0 + 1)
            for j in range(1, BLK):
                hidden(j, j)
            with loop(ET.Activation, 0, NBLK - 1) as b:
                for m in range(BLK):
                    split_hi(W2_0 + m + 2, 16 * b)
                for j in range(BLK):
                    act.wait_ge(unit_done, 16 * b + (W2_0 + BLK + j + 1))
                    hidden(BLK + j, j % 2, 8 * b)
                    split_hi(W2_0 + BLK + j + 2, 16 * b)

            q = W2_0 + 16 * (NBLK - 1)
            for m in range(BLK):
                if m < BLK - 2:
                    split_hi(q + m + 2)
                for n in (2 * m, 2 * m + 1):
                    act.wait_ge(x2_done, 16 * (NBLK - 1) + n + 2)
                    if n:
                        act.wait_ge(ss2_done, n)
                    act.activation(sq[:], ch(xb, n), ACT.Square).then_inc(x2sq_done, 1)
            root(4)

        @block.vector
        def _(dve):
            steps = [0]

            def chain(ins):
                steps[0] += 1
                ins.then_inc(dv, 1)
                dve.wait_ge(dv, steps[0])

            dve.memset(ones[:], 1.0).then_inc(ones_set, 1)
            dve.memset(acc1[:, 0:1], 0.0).then_inc(conv_done, 1)
            dve.wait_ge(par_in, 16)
            dve.tensor_scalar(b1p[:, 0:KC], pr[:, COL["ada_b"]:COL["ada_b"] + 2 * KC:2], 1.0, None, ALU.add
                              ).then_inc(small, 1)
            dve.tensor_scalar(b1p[:, KC:2 * KC], col("ada_b", M_SC2, KC), 1.0, None, ALU.add).then_inc(small, 1)

            def variance(bank):
                chain(dve.tensor_scalar(tb[:], ps[:, bank, :], 1.0 / D, EPS, ALU.mult, ALU.add))
                dve.reciprocal(ta[:], tb[:]).then_inc(var_done, 1)

            dve.wait_ge(xsq_used, KC)
            variance(7)
            dve.wait_ge(cs_ready, 1)

            def ada_reduce(a, off=0):
                wait_ada(dve, a, off)
                s = adar[:, a % 2, :]
                dve.scalar_tensor_tensor(s, s, 1.0, csb[:], ALU.mult, ALU.mult,
                                         accum_out=mod[:, bass.ds(a + off, 1)]).then_inc(ada_used, 1)

            def lo_part(k, n, src):
                dve.wait_ge(hhi_done, n + 1)
                dve.tensor_tensor(ch(hlo, k), src[:], f(ch(hhi, k)), ALU.subtract).then_inc(hlo_done, 1)

            def a0_chunk(k):
                first = isinstance(k, int)
                ada_reduce(0, 2 * k)
                if not first:
                    lo_part(k - 1, k - 1, tb)
                ada_reduce(1, 2 * k)
                if first:
                    dve.wait_ge(rstd_done, 1)
                dve.tensor_tensor(ta[:], ch(xb, k), rstd[:], ALU.mult).then_inc(dv, 1)
                dve.wait_ge(ada_used, 2 * k + 2)
                dve.wait_ge(small, 2 * k + 2)
                dve.scalar_tensor_tensor(modb[:, bass.ds(2 * k, 1)], mod[:, bass.ds(2 * k, 1)],
                                         b1p[:, bass.ds(k, 1)], col("norm1_g", k), ALU.add, ALU.mult
                                         ).then_inc(small, 1)
                dve.tensor_tensor(modb[:, bass.ds(2 * k + 1, 1)], mod[:, bass.ds(2 * k + 1, 1)],
                                  col("ada_b", 2 * k + 1), ALU.add).then_inc(small, 1)
                dve.wait_ge(small, 2 * k + 4)
                dve.wait_ge(dv, k + (steps[0] + 1))
                dve.tensor_scalar(tb[:], ta[:], modb[:, bass.ds(2 * k, 1)], modb[:, bass.ds(2 * k + 1, 1)],
                                  ALU.mult, ALU.add).then_inc(hf_ready, 1)

            a0_chunk(0)
            with loop(ET.DVE, 1, KC) as k:
                a0_chunk(k)
            lo_part(KC - 1, KC - 1, tb)
            steps[0] += KC
            n_small = 2 + 2 * KC

            def glu(c, bank):
                dve.wait_ge(sig_done, c + 1)
                dve.scalar_tensor_tensor(ch(xb, c), ps[:, bank, :], col("b_in", c), sig[:], ALU.add, ALU.mult
                                         ).then_inc(glu_done, 1)

            def conv(c, bank, n0):
                acc0 = ps[:, bank, :]

                def tap(j):
                    return col("w_dw", c * TAPS + j)

                dve.wait_ge(glu_done, c + 1)
                dve.tensor_scalar(acc0, ch(xb, c), tap(30), col("b_dw", c), ALU.mult, ALU.add).then_inc(dv, 1)
                dve.wait_ge(conv_done, c + 1)
                dve.tensor_scalar(acc1[:, 1:T], ch(xb, c, 0, T - 1), tap(29), None, ALU.mult).then_inc(dv, 1)
                n = 2
                for j in range(28, -1, -1):
                    s = TAPS - 1 - j
                    acc = acc1[:, s:T] if j % 2 else acc0[:, s:T]
                    dve.wait_ge(dv, n0 + (n - 1))
                    dve.scalar_tensor_tensor(acc, ch(xb, c, 0, T - s), tap(j), acc, ALU.mult, ALU.add
                                             ).then_inc(dv, 1)
                    n += 1
                dve.wait_ge(dv, n0 + n)
                dve.tensor_tensor(ch(xb, c), acc0, acc1[:], ALU.add).then_inc(conv_done, 1)

            for c in range(4):
                glu(c, 2 * c)
            with loop(ET.DVE, 0, 6) as i:
                for s in range(2):
                    conv(2 * i + s, 4 + s, 2 * TAPS * i + (steps[0] + TAPS * s))
                    glu(2 * i + (4 + s), 2 * s)
            steps[0] += 12 * TAPS
            for c in range(12, KC):
                conv(c, 4 + c % 2, steps[0])
                steps[0] += TAPS

            dve.wait_ge(stat_done, 1)
            chain(dve.tensor_scalar(mu[:], ps[:, 6, :], 1.0 / D, None, ALU.mult))
            chain(dve.tensor_tensor(ta[:], mu[:], mu[:], ALU.mult))
            dve.wait_ge(stat_done, 2)
            chain(dve.scalar_tensor_tensor(tb[:], ps[:, 7, :], 1.0 / D, ta[:], ALU.mult, ALU.subtract))
            chain(dve.tensor_scalar(tb[:], tb[:], 0.0, EPS, ALU.max, ALU.add))
            dve.reciprocal(ta[:], tb[:]).then_inc(var_done, 1)
            dve.wait_ge(ada_used, 2 * KC + ADA_A1)
            dve.tensor_tensor(modb[:, M_G1:M_G1 + KC], mod[:, M_G1:M_G1 + KC], col("ada_b", M_G1, KC), ALU.add
                              ).then_inc(small, 1)
            dve.wait_ge(small, n_small + 1)
            dve.tensor_tensor(g1b[:], modb[:, M_G1:M_G1 + KC], col("b_out", 0, KC), ALU.mult).then_inc(small, 1)
            assert n_small + 2 == SMALL_G1

            def z(k):
                dve.wait_ge(hf_ready, KC + k)
                chain(dve.tensor_tensor(ta[:], ch(xb, k), mu[:], ALU.subtract))
                if k:
                    lo_part(k - 1, KC + k - 1, sq)
                dve.tensor_tensor(tb[:], ta[:], rstd[:], ALU.mult).then_inc(hf_ready, 1)

            def split_lo(q, off=0):
                dve.wait_ge(whi_done, q + 1 + off)
                dve.tensor_tensor(wlo[:, q % WS, :], raw[:, q % RAW, :], f(whi[:, q % WS, :]), ALU.subtract
                                  ).then_inc(wlo_done, 1)

            dve.wait_ge(rstd_done, 2)
            for k in range(4):
                z(k)
            a = 2 * KC + ADA_A1
            dve.wait_ge(wlo_done, LO_POOL)
            for j in range(7):
                for k in (4 + 2 * j, 5 + 2 * j):
                    if k < KC:
                        z(k)
                if j == 5:
                    lo_part(KC - 1, 2 * KC - 1, sq)
                if j:
                    split_lo(B0 + 1 + j)
                if j % 2:
                    for _ in range(3):
                        ada_reduce(a)
                        a += 1
            split_lo(B0 + 8)

            def x1(n):
                dve.wait_ge(yg_done, n + 1)
                dve.wait_ge(xr_in[n // 4], 16)
                dve.tensor_tensor(ch(xb, n), sig[:], ch(xb, n), ALU.add).then_inc(x1_done, 1)

            def add_squares(n, done, seen, base):
                dve.wait_ge(seen, base + n + 1)
                if n == 0:
                    dve.tensor_copy(ssum[:], sq[:]).then_inc(done, 1)
                else:
                    dve.wait_ge(done, n)
                    dve.tensor_tensor(ssum[:], ssum[:], sq[:], ALU.add).then_inc(done, 1)

            x1(0)
            x1(1)
            split_lo(B1 + 1)
            for n in range(2, 8):
                x1(n)
                add_squares(n - 2, ss1_done, x1sq_done, 0)
            add_squares(6, ss1_done, x1sq_done, 0)
            for _ in range(3):
                ada_reduce(a)
                a += 1
            for j in range(8):
                x1(8 + j)
                split_lo(B1 + j + 2)
                add_squares(7 + j, ss1_done, x1sq_done, 0)
                if j < 7:
                    for _ in range(2):
                        ada_reduce(a)
                        a += 1
            add_squares(15, ss1_done, x1sq_done, 0)
            dve.wait_ge(ada_used, M_G2)
            dve.scalar_tensor_tensor(modb[:, M_SC2:M_SC2 + KC], mod[:, M_SC2:M_SC2 + KC], 1.0, b1p[:, KC:2 * KC],
                                     ALU.mult, ALU.add).then_inc(small, 1)
            dve.tensor_tensor(modb[:, M_SH2:M_SH2 + KC], mod[:, M_SH2:M_SH2 + KC], col("ada_b", M_SH2, KC), ALU.add
                              ).then_inc(small, 1)
            dve.wait_ge(small, SMALL_G1 + 2)
            dve.tensor_tensor(modb[:, M_SC2:M_SC2 + KC], modb[:, M_SC2:M_SC2 + KC], col("norm2_g", 0, KC), ALU.mult
                              ).then_inc(small, 1)
            dve.wait_ge(small, SMALL_G1 + 3)
            dve.wait_ge(stat_done, 3)
            variance(2)

            def h2(k):
                dve.wait_ge(hf_ready, 2 * KC + k)
                chain(dve.tensor_tensor(ta[:], ch(xb, k), rstd[:], ALU.mult))
                if k:
                    lo_part(k - 1, 2 * KC + k - 1, tb)
                    dve.wait_ge(hlo_done, 2 * KC + k)
                dve.tensor_scalar(tb[:], ta[:], modb[:, M_SC2 + k:M_SC2 + k + 1], modb[:, M_SH2 + k:M_SH2 + k + 1],
                                  ALU.mult, ALU.add).then_inc(hf_ready, 1)

            dve.wait_ge(rstd_done, 3)
            for k in range(4):
                h2(k)
            for j in range(7):
                for k in (4 + 2 * j, 5 + 2 * j):
                    if k < KC:
                        h2(k)
                if j == 5:
                    lo_part(KC - 1, 3 * KC - 1, tb)
                if j:
                    split_lo(C0 + 1 + j)
                for _ in range(2):
                    if a < ADA:
                        ada_reduce(a)
                        a += 1
            split_lo(C0 + 8)
            while a < ADA:
                ada_reduce(a)
                a += 1
            dve.wait_ge(ada_used, ADA)
            dve.tensor_tensor(modb[:, M_G2:M_G2 + KC], mod[:, M_G2:M_G2 + KC], col("ada_b", M_G2, KC), ALU.add
                              ).then_inc(x2_done, 1)

            def hidden_lo(j, off=0):
                dve.wait_ge(dhi_done, j + 1 + off)
                dve.tensor_tensor(ch(dlo, j % BLK), sq[:], f(ch(dhi, j % BLK)), ALU.subtract).then_inc(dlo_done, 1)

            def x2(m, off=0):
                for nn in range(2):
                    n = 2 * m + nn
                    dve.scalar_tensor_tensor(ch(xb, n), ps[:, 4 + 2 * (m % 2) + nn, :],
                                             modb[:, M_G2 + n:M_G2 + n + 1], ch(xb, n), ALU.mult, ALU.add
                                             ).then_inc(x2_done, 1)

            hidden_lo(0)
            split_lo(W2_0 + 1)
            for j in range(1, BLK):
                hidden_lo(j)
            with loop(ET.DVE, 0, NBLK - 1) as b:
                for m in range(BLK):
                    dve.wait_ge(unit_done, 16 * b + (W2_0 + m + 1))
                    if m == 0:
                        dve.wait_ge(x2_done, 16 * b + 1)
                    x2(m)
                    split_lo(W2_0 + m + 2, 16 * b)
                for j in range(BLK):
                    hidden_lo(BLK + j, 8 * b)
                    split_lo(W2_0 + BLK + j + 2, 16 * b)
            q = W2_0 + 16 * (NBLK - 1)
            for m in range(BLK):
                dve.wait_ge(unit_done, q + m + 1)
                if m == 0:
                    dve.wait_ge(x2_done, 16 * (NBLK - 1) + 1)
                x2(m)
                if m < BLK - 2:
                    split_lo(q + m + 2)
                add_squares(2 * m, ss2_done, x2sq_done, 0)
                add_squares(2 * m + 1, ss2_done, x2sq_done, 0)
            dve.wait_ge(stat_done, 4)
            variance(2)
            dve.wait_ge(rstd_done, 4)
            for n in range(KC):
                dve.scalar_tensor_tensor(ch(xb, n), ch(xb, n), col("final_g", n), rstd[:], ALU.mult, ALU.mult
                                         ).then_inc(fin_done, 1)

        @block.gpsimd
        def _(pool):
            def split_lo(q, off=0):
                pool.wait_ge(whi_done, q + 1 + off)
                pool.tensor_tensor(wlo[:, q % WS, :], raw[:, q % RAW, :], f(whi[:, q % WS, :]), ALU.subtract
                                   ).then_inc(wlo_done, 1)

            def c_sums(c):
                pool.wait_ge(conv_done, c + 2)
                pool.wait_ge(s1_done, c + 1)
                pool.tensor_tensor(s1[:], s1[:], ch(xb, c), ALU.add).then_inc(s1_done, 1)
                pool.wait_ge(csq_done, c + 1)
                pool.wait_ge(s2_done, c + 1)
                pool.tensor_tensor(s2[:], s2[:], sq[:], ALU.add).then_inc(s2_done, 1)

            pool.memset(s1[:], 0.0).then_inc(s1_done, 1)
            pool.memset(s2[:], 0.0).then_inc(s2_done, 1)
            for q in range(A0, A1 + 2):
                split_lo(q)
            pool.wait_ge(ada_used, 2 * KC)
            pool.wait_ge(cs_ready, 1)
            with loop(ET.Pool, 0, 6) as i:
                for s in range(2):
                    split_lo(A1 + 2 + 2 * s, 4 * i)
                    split_lo(A1 + 3 + 2 * s, 4 * i)
                    for a in (2 * KC + 2 * s, 2 * KC + 2 * s + 1):
                        wait_ada(pool, a, 4 * i)
                        pool.tensor_tensor(adar[:, a % 2, :], adar[:, a % 2, :], csb[:], ALU.mult
                                           ).then_inc(ada_mul, 1)
                    c_sums(2 * i + s)
            for c in range(12, KC):
                c_sums(c)


def _tiles(m, rows, cols):
    t = m.reshape(m.shape[0] // P, P, m.shape[1] // P, P)[rows][:, :, cols]
    return t.transpose(1, 0, 2, 3).reshape(P, -1)


def _units(w_in, w_out, w1, w2):
    every = list(range(KC))
    in_cols = [h * KC + c for c in range(4) for h in range(2)]
    for j in range(8):
        yield _tiles(w_in, [2 * j, 2 * j + 1], in_cols)
    for c in range(4, KC):
        for h in range(2):
            yield _tiles(w_in, every, [h * KC + c])
    for j in range(8):
        yield _tiles(w_out, [2 * j, 2 * j + 1], list(range(8)))
    for j in range(8):
        yield _tiles(w_out, every, [8 + j])
    for b in range(NBLK):
        for j in range(BLK):
            if b == 0:
                yield _tiles(w1, [2 * j, 2 * j + 1], list(range(8)))
            else:
                yield _tiles(w1, every, [BLK * b + j])
        rows = list(range(BLK * b, BLK * (b + 1)))
        for m in range(BLK):
            yield np.concatenate([_tiles(w2, rows, [2 * m + nn]) for nn in range(2)], axis=1)


def kernel(x, c, ada_w, ada_b, norm1_g, norm2_g, mlp_w1, mlp_w2, final_g, conv_w_in, conv_b_in, conv_w_dw,
           conv_b_dw, conv_ln_g, conv_ln_b, conv_w_out, conv_b_out, **other_mixers):
    import concourse.bacc as bacc
    from concourse.bass_utils import run_bass_kernel_spmd

    def chunks(v):
        return np.asarray(v).reshape(-1, P).T

    order = [h * KC + k for k in range(KC) for h in (1, 0)]
    order += [part * KC + k for part in (2, 4, 3, 5) for k in range(KC)]
    w = np.stack(list(_units(np.asarray(conv_w_in)[0], np.asarray(conv_w_out)[0],
                             np.asarray(mlp_w1)[0], np.asarray(mlp_w2)[0])))
    ada = np.ascontiguousarray(np.asarray(ada_w)[0].T.reshape(ADA, P, D)[order])
    dw = np.asarray(conv_w_dw)[0].T.reshape(KC, P, TAPS).transpose(1, 0, 2).reshape(P, -1)
    packed = {"ada_b": chunks(np.asarray(ada_b)[0])[:, order], "norm1_g": chunks(norm1_g), "norm2_g": chunks(norm2_g),
              "final_g": chunks(final_g), "b_in": chunks(conv_b_in), "b_dw": chunks(conv_b_dw),
              "ln_g": chunks(conv_ln_g), "ln_b": chunks(conv_ln_b), "b_out": chunks(conv_b_out), "w_dw": dw}
    arrays = {
        "xT": np.ascontiguousarray(np.asarray(x)[0].T),
        "c": np.ascontiguousarray(np.asarray(c)[0]),
        "w": w,
        "ada": ada,
        "par": np.ascontiguousarray(np.concatenate([packed[name] for name, _ in PARAMS], axis=1)),
    }
    nc = bacc.Bacc("TRN2", target_bir_lowering=False, num_devices=1)
    aps = {n: nc.dram_tensor(n, a.shape, F32, kind="ExternalInput").ap() for n, a in arrays.items()}
    out = nc.dram_tensor("out", (D, T), F32, kind="ExternalOutput").ap()
    trunk_kernel(nc, aps["xT"], aps["c"], aps["w"].rearrange("q p n -> p q n"),
                 aps["ada"].rearrange("a p n -> p a n"), aps["par"], out)
    r = run_bass_kernel_spmd(nc, [arrays], core_ids=[0])
    return np.ascontiguousarray(r.results[0]["out"].T).reshape(1, T, D)
```

```python
from contextlib import ExitStack

import numpy as np

import concourse.bass as bass
from concourse import mybir

F32 = mybir.dt.float32
F32R = mybir.dt.float32r
ALU = mybir.AluOpType
ACT = mybir.ActivationFunctionType
ET = mybir.EngineType

P = 128
D = 2048
T = 512
KC = D // P
FF = 4 * D
BLK = 8
NBLK = FF // P // BLK
TAPS = 31
EPS = 1e-6
TILES = 16
U = TILES * P
RAW = 4
WS = 2

A0, A1, B0, B1, C0, W2_0 = 0, 8, 32, 40, 48, 56
NUNITS = C0 + 2 * BLK * NBLK
LO_POOL = W2_0 + 2

M_G1, M_SC2, M_SH2, M_G2 = 2 * KC, 3 * KC, 4 * KC, 5 * KC
ADA = 6 * KC
ADA_A1, ADA_B0, ADA_B1, ADA_C0 = 12, 18, 18, 16

FIN_POOL = 11
SMALL_G1 = 2 * KC + 4

PARAMS = [("ada_b", ADA), ("norm1_g", KC), ("norm2_g", KC), ("final_g", KC), ("b_in", 2 * KC), ("b_dw", KC),
          ("ln_g", KC), ("ln_b", KC), ("b_out", KC), ("w_dw", KC * TAPS)]
COL, _n = {}, 0
for _name, _w in PARAMS:
    COL[_name] = _n
    _n += _w
NPAR = _n


def trunk_kernel(nc, xT, c, w, ada, par, out):
    x_d = xT.rearrange("(k p) t -> p k t", p=P)
    out_d = out.rearrange("(k p) t -> p k t", p=P)

    with ExitStack() as ctx:
        def sb(name, shape, dt=F32, scope=ctx):
            return scope.enter_context(nc.sbuf_tensor(name, shape, dt))

        def sem(name):
            return ctx.enter_context(nc.semaphore(name))

        xb = sb("xb", [P, KC * T])
        hhi = sb("hhi", [P, KC * T], F32R)
        hlo = sb("hlo", [P, KC * T], F32R)
        raw = sb("raw", [P, RAW, U])
        whi = sb("whi", [P, WS, U], F32R)
        wlo = sb("wlo", [P, WS, U], F32R)
        pr = sb("pr", [P, NPAR])
        mod = sb("mod", [P, ADA])
        modb = sb("modb", [P, ADA])
        b1p = sb("b1p", [P, 2 * KC])
        g1b = sb("g1b", [P, KC])
        rstd = sb("rstd", [P, T])
        ta = sb("ta", [P, T])
        tb = sb("tb", [P, T])
        sq = sb("sq", [P, T])
        ssum = sb("ssum", [P, T])
        st = sb("st", [P, 16])
        ones = sb("ones", [P, 1])
        ident = sb("ident", [P, P])
        dump = sb("dump", [P, 1])
        with ExitStack() as early:
            csb = sb("csb", [P, D], scope=early)
            adar = sb("adar", [P, 2, D], scope=early)
            sig = sb("sig", [P, T], scope=early)
            pacc = sb("pacc", [P, T], scope=early)
            s1 = sb("s1", [P, T], scope=early)
            s2 = sb("s2", [P, T], scope=early)
        dhi = sb("dhi", [P, BLK * T], F32R)
        dlo = sb("dlo", [P, BLK * T], F32R)
        ps = ctx.enter_context(nc.psum_tensor("ps", [P, 8, T], F32))
        mu = ssum
        scaled, normed, silus = (ta, s1), (tb, s2), (sq, pacc)
        relus, squares = (ta, tb), (sq, ssum)

        def f(ap):
            return ap.bitcast(F32)

        def ch(buf, k, lo=0, n=T):
            return buf[:, bass.ds(k * T + lo, n)]

        def col(name, k, n=1):
            return pr[:, bass.ds(COL[name] + k, n)]

        x_in = [sem(f"x_in{i}") for i in range(4)]
        xr_in = [sem(f"xr_in{i}") for i in range(4)]
        c_in, par_in = sem("c_in"), sem("par_in")
        raw_in = [sem(f"raw_in{i}") for i in range(RAW)]
        ada_in = [sem(f"ada_in{i}") for i in range(2)]
        out_done = sem("out_done")
        ones_set, ident_clear, ident_set = sem("ones_set"), sem("ident_clear"), sem("ident_set")
        cs_ready = sem("cs_ready")
        whi_done = sem("whi_done")
        wlo_done = sem("wlo_done")
        unit_done = sem("unit_done")
        ada_mul = sem("ada_mul")
        ada_used = sem("ada_used")
        small = sem("small")
        xsq_done = sem("xsq_done")
        xsq_used = sem("xsq_used")
        stat_done = sem("stat_done")
        var_done = sem("var_done")
        root_done = sem("root_done")
        spread_done = sem("spread_done")
        rstd_done = sem("rstd_done")
        warm = sem("warm")
        dv = sem("dv")
        ac = sem("ac")
        hf_ready = sem("hf_ready")
        hhi_done = sem("hhi_done")
        hlo_done = sem("hlo_done")
        sig_done = sem("sig_done")
        glu_done = sem("glu_done")
        conv_done = sem("conv_done")
        csq_done = sem("csq_done")
        s1_done = sem("s1_done")
        s2_done = sem("s2_done")
        yg_done = sem("yg_done")
        x1_done = sem("x1_done")
        x1sq_done = sem("x1sq_done")
        ss1_done = sem("ss1_done")
        relu_done = sem("relu_done")
        dsq_done = sem("dsq_done")
        dhi_done = sem("dhi_done")
        dlo_done = sem("dlo_done")
        x2_done = sem("x2_done")
        x2sq_done = sem("x2sq_done")
        ss2_done = sem("ss2_done")
        fg_done = sem("fg_done")
        fin_dve = sem("fin_dve")
        fin_pool = sem("fin_pool")

        block = ctx.enter_context(nc.Block())

        def loop(eng, n0, n1):
            return nc.Fori(n0, n1, engines=(eng,))

        def ada_share(n, j):
            return (j + 1) * n // 8 - j * n // 8

        def wait_raw(eng, q, off=0):
            eng.wait_ge(raw_in[q % RAW], 16 * (q // RAW + 1) + (16 // RAW) * off)

        def wait_ada(eng, a, off=0):
            eng.wait_ge(ada_in[a % 2], 16 * (a // 2 + 1) + 8 * off)

        @block.sync
        def _(sp):
            sp.dma_start(csb[:], c.partition_broadcast(P)).then_inc(c_in, 16)
            sp.dma_start(pr[:], par).then_inc(par_in, 16)
            for i in range(4):
                sp.dma_start(xb[:, 4 * i * T:4 * (i + 1) * T].rearrange("p (k t) -> p k t", t=T),
                             x_d[:, 4 * i:4 * i + 4, :]).then_inc(x_in[i], 16)

            def load_unit(q, off=0):
                if q >= RAW:
                    sp.wait_ge(wlo_done, q - RAW + 1 + off)
                sp.dma_start(raw[:, q % RAW:q % RAW + 1, :], w[:, bass.ds(q + off, 1), :]
                             ).then_inc(raw_in[q % RAW], 16)

            def load_ada(a, off=0):
                if a >= 2:
                    sp.wait_ge(ada_used, a - 1 + off)
                sp.dma_start(adar[:, a % 2:a % 2 + 1, :], ada[:, bass.ds(a + off, 1), :]
                             ).then_inc(ada_in[a % 2], 16)

            a = 0
            for q in range(A0, A1):
                for _ in range(4):
                    load_ada(a)
                    a += 1
                load_unit(q)
            load_unit(A1)
            load_unit(A1 + 1)
            with loop(ET.SP, 0, 6) as i:
                for s in range(2):
                    load_unit(A1 + 2 + 2 * s, 4 * i)
                    load_unit(A1 + 3 + 2 * s, 4 * i)
                    load_ada(2 * KC + s, 2 * i)
            a += ADA_A1

            def x_again(g):
                sp.wait_ge(hf_ready, KC + 4 * g + 4)
                sp.dma_start(xb[:, 4 * g * T:4 * (g + 1) * T].rearrange("p (k t) -> p k t", t=T),
                             x_d[:, 4 * g:4 * g + 4, :]).then_inc(xr_in[g], 16)

            for q0, n_ada in ((B0, ADA_B0), (B1, ADA_B1), (C0, ADA_C0)):
                for j in range(8):
                    load_unit(q0 + 2 + j)
                    for _ in range(ada_share(n_ada, j)):
                        load_ada(a)
                        a += 1
                    if q0 == B0 and j % 2 and j > 1:
                        x_again(j // 2 - 1)
                if q0 == B0:
                    x_again(3)
            assert a == ADA
            load_unit(W2_0 + 2)
            load_unit(W2_0 + 3)
            with loop(ET.SP, 1, (NUNITS - W2_0) // RAW) as i:
                for q in range(RAW):
                    load_unit(W2_0 + q, 4 * i)
            stores = [(fin_dve, n, min(2, FIN_POOL - n)) for n in range(0, FIN_POOL, 2)]
            for i, n in enumerate(range(FIN_POOL, KC)):
                stores.insert(2 * i + 1, (fin_pool, n, 1))
            for done, n, m in stores:
                sp.wait_ge(done, n + m - (FIN_POOL if done is fin_pool else 0))
                sp.dma_start(out_d[:, n:n + m, :], xb[:, n * T:(n + m) * T].rearrange("p (k t) -> p k t", t=T)
                             ).then_inc(out_done, 16)
            sp.wait_ge(out_done, 16 * len(stores))

        @block.tensor
        def _(pe):
            def product(bank, slot, tile, xhi, xlo, first, last):
                t = slice(tile * P, (tile + 1) * P)
                out = ps[:, bank, :]
                pe.matmul(out, whi[:, slot, t], xhi, start=first, stop=False, skip_group_check=True)
                pe.matmul(out, whi[:, slot, t], xlo, start=False, stop=False, skip_group_check=True)
                return pe.matmul(out, wlo[:, slot, t], xhi, start=False, stop=last, skip_group_check=True)

            def outer_unit(q, s, h0, i=None):
                i, first = (0, s == 0) if i is None else (i, False)
                pe.wait_ge(wlo_done, 2 * i + (q + s + 1))
                for kk in range(2):
                    k = 4 * i + (2 * s + kk)
                    pe.wait_ge(hlo_done, k + (h0 + 1))
                    for o in range(8):
                        last = product(o, s, 8 * kk + o, ch(hhi, k), ch(hlo, k), first and kk == 0, False)
                last.then_inc(unit_done, 1)

            def outer_units(q, h0):
                for s in range(2):
                    outer_unit(q, s, h0)
                with loop(ET.PE, 1, 4) as i:
                    for s in range(2):
                        outer_unit(q, s, h0, i)

            def inner_unit(slot, bank, seen):
                pe.wait_ge(wlo_done, seen)
                for k in range(KC):
                    last = product(bank, slot, k, ch(hhi, k), ch(hlo, k), k == 0, k == KC - 1)
                last.then_inc(unit_done, 1)

            def token_sums(bank, col0, src, start):
                for j in range(T // P):
                    last = pe.matmul(ps[:, bank, col0 + j:col0 + j + 1], src[:, j * P:(j + 1) * P], ones[:],
                                     start=start and j == 0, stop=False, skip_group_check=True)
                return last

            def spread(bank, col0):
                for j in range(T // P):
                    last = pe.matmul(ps[:, bank, j * P:(j + 1) * P], st[:, col0 + j:col0 + j + 1].to_broadcast([P, P]),
                                     ident[:], start=j == 0, stop=False, skip_group_check=True)
                last.then_inc(spread_done, 1)

            pe.wait_ge(ones_set, 1)
            for k in range(KC):
                pe.wait_ge(xsq_done, k + 1)
                token_sums(6, 0, sq if k % 2 else sig, k == 0).then_inc(xsq_used, 1)
            pe.wait_ge(ident_set, 1)
            pe.wait_ge(root_done, 1)
            spread(7, 8)
            pe.wait_ge(rstd_done, 1)
            outer_units(A0, 0)
            with loop(ET.PE, 0, 6) as i:
                for s in range(2):
                    pe.wait_ge(glu_done, 2 * i + (3 + s))
                    inner_unit(0, 2 * s, 4 * i + (A1 + 2 * s + 1))
                    inner_unit(1, 2 * s + 1, 4 * i + (A1 + 2 * s + 2))
            pe.wait_ge(s1_done, KC + 1)
            token_sums(0, 0, s1, True)
            pe.wait_ge(s2_done, KC + 1)
            token_sums(0, 4, s2, False).then_inc(stat_done, 1)
            pe.wait_ge(root_done, 2)
            spread(1, 8)
            spread(2, 12)
            outer_units(B0, KC)
            for s in range(2):
                pe.wait_ge(yg_done, s + 1)
                inner_unit(s, s, B1 + s + 1)
            with loop(ET.PE, 1, 4) as i:
                for s in range(2):
                    pe.wait_ge(yg_done, 2 * i + (7 + s))
                    inner_unit(s, s, 2 * i + (B1 + s + 1))
            pe.wait_ge(ss1_done, KC)
            token_sums(2, 0, ssum, True).then_inc(stat_done, 1)
            pe.wait_ge(root_done, 3)
            spread(3, 8)
            outer_units(C0, 2 * KC)

            def w2_unit(m, seen, wait_hidden=None):
                pe.wait_ge(wlo_done, seen)
                for nn in range(2):
                    for k in range(BLK):
                        if wait_hidden is not None and nn == 0:
                            pe.wait_ge(dlo_done, wait_hidden + (k + 1))
                        last = product(4 + 2 * (m % 2) + nn, m % 2, 8 * nn + k, ch(dhi, k), ch(dlo, k),
                                       k == 0, k == BLK - 1)
                last.then_inc(unit_done, 1)

            def w2_block(b):
                pe.wait_ge(x2_done, 16 * b + 1)
                pe.wait_ge(relu_done, 8 * b + 6)
                w2_unit(0, 16 * b + (W2_0 + 1), 8 * b)
                w2_unit(1, 16 * b + (W2_0 + 2))
                with loop(ET.PE, 1, 4) as i:
                    for s in range(2):
                        pe.wait_ge(x2_done, 16 * b + 4 * i + (2 * s - 1))
                        w2_unit(s, 16 * b + 2 * i + (W2_0 + s + 1))

            with loop(ET.PE, 0, NBLK - 1) as b:
                w2_block(b)
                with loop(ET.PE, 0, 4) as i:
                    for s in range(2):
                        pe.wait_ge(relu_done, 8 * b + 2 * i + (BLK + s - 1))
                        inner_unit(s, s, 16 * b + 2 * i + (W2_0 + BLK + s + 1))
            w2_block(NBLK - 1)
            pe.wait_ge(ss2_done, KC)
            token_sums(0, 0, ssum, True).then_inc(stat_done, 1)
            pe.wait_ge(root_done, 4)
            spread(1, 8)

        @block.scalar
        def _(act):
            def split_hi(q, off=0):
                wait_raw(act, q, off)
                if q >= WS:
                    act.wait_ge(unit_done, q - WS + 1 + off)
                act.activation(whi[:, q % WS, :], raw[:, q % RAW, :], ACT.Copy).then_inc(whi_done, 1)

            def preload(func):
                act.wait_ge(ones_set, 1)
                act.activation(dump[:], ones[:], func).then_inc(warm, 1)

            def root(n, bank, mean_bank=None):
                act.wait_ge(var_done, n)
                act.activation(st[:, 8:12], st[:, 4:8], ACT.Sqrt).then_inc(root_done, 1)
                if mean_bank is not None:
                    preload(ACT.Silu)
                act.wait_ge(spread_done, n + (n > 2))
                act.activation(rstd[:], ps[:, bank, :], ACT.Copy).then_inc(rstd_done, 1)
                if mean_bank is not None:
                    act.wait_ge(spread_done, n + 1)
                    act.activation(mu[:], ps[:, mean_bank, :], ACT.Copy).then_inc(rstd_done, 1)

            def h_hi(k, n, src):
                act.wait_ge(hf_ready, n + 1)
                act.activation(ch(hhi, k), src[:], ACT.Copy).then_inc(hhi_done, 1)

            act.wait_ge(c_in, 16)
            act.activation(csb[:], csb[:], ACT.Silu).then_inc(cs_ready, 1)
            preload(ACT.Sqrt)
            for k in range(KC):
                act.wait_ge(x_in[k // 4], 16)
                if k >= 2:
                    act.wait_ge(xsq_used, k - 1)
                act.activation((sq if k % 2 else sig)[:], ch(xb, k), ACT.Square).then_inc(xsq_done, 1)
            root(1, 7)
            preload(ACT.Sigmoid)
            for j in range(8):
                h_hi(2 * j, 2 * j, tb)
                split_hi(j)
                h_hi(2 * j + 1, 2 * j + 1, tb)

            act.wait_ge(par_in, 16)

            def sigmoid(c, bank, n):
                act.wait_ge(glu_done, n)
                act.activation(sig[:], ps[:, bank, :], ACT.Sigmoid, bias=col("b_in", c + KC)).then_inc(sig_done, 1)

            def c_square(c):
                act.wait_ge(conv_done, c + 2)
                act.wait_ge(s2_done, c + 1)
                act.activation(sq[:], ch(xb, c), ACT.Square).then_inc(csq_done, 1)

            split_hi(8)
            act.wait_ge(unit_done, A1)
            for c in range(4):
                sigmoid(c, 2 * c + 1, c)
                if c == 0:
                    split_hi(9)

            def ada_sum(a, off):
                act.wait_ge(ada_mul, a - 2 * KC + 1 + off)
                act.activation(adar[:, a % 2, :], adar[:, a % 2, :], ACT.Copy,
                               accum_out=mod[:, bass.ds(a + off, 1)]).then_inc(ada_used, 1)

            with loop(ET.Activation, 0, 6) as i:
                for s in range(2):
                    split_hi(A1 + 2 + 2 * s, 4 * i)
                    split_hi(A1 + 3 + 2 * s, 4 * i)
                    act.wait_ge(unit_done, 4 * i + (A1 + 2 * s + 2))
                    sigmoid(2 * i + (4 + s), 2 * s + 1, 2 * i + (4 + s))
                    ada_sum(2 * KC + s, 2 * i)
                    c_square(2 * i + s)
            preload(ACT.Sqrt)
            for c in range(12, KC):
                c_square(c)
            root(2, 1, 2)

            def z(k):
                if k < KC:
                    act.wait_ge(hf_ready, KC + k + 1)
                    if k >= 2:
                        act.wait_ge(hlo_done, KC + k - 1)
                    act.activation(silus[k % 2][:], normed[k % 2][:], ACT.Silu, scale=col("ln_g", k),
                                   bias=col("ln_b", k)).then_inc(ac, 1)
                if k:
                    act.wait_ge(ac, k)
                    act.activation(ch(hhi, k - 1), silus[(k - 1) % 2][:], ACT.Copy).then_inc(hhi_done, 1)

            for k in range(4):
                z(k)
            for j in range(7):
                split_hi(B0 + 2 + j)
                for k in range(4 * j + 4, 4 * j + 8):
                    if k <= KC:
                        z(k)

            def gated(n, bank):
                if n:
                    act.wait_ge(x1_done, n)
                act.activation(sig[:], ps[:, bank, :], ACT.Identity, scale=modb[:, M_G1 + n:M_G1 + n + 1],
                               bias=g1b[:, n:n + 1]).then_inc(yg_done, 1)

            def x1_square(n):
                act.wait_ge(x1_done, n + 1)
                if n:
                    act.wait_ge(ss1_done, n)
                act.activation(sq[:], ch(xb, n), ACT.Square).then_inc(x1sq_done, 1)

            act.wait_ge(small, SMALL_G1)
            act.wait_ge(unit_done, B1)
            gated(0, 0)
            gated(1, 1)
            split_hi(B1 + 1)
            for n in range(2, 8):
                gated(n, n)
                x1_square(n - 2)
            x1_square(6)
            for j in range(8):
                n = 8 + j
                if j == 7:
                    preload(ACT.Sqrt)
                act.wait_ge(unit_done, B1 + j + 1)
                gated(n, j % 2)
                split_hi(B1 + j + 2)
                x1_square(n - 1)
            x1_square(15)
            root(3, 3)
            for k in range(4):
                h_hi(k, 2 * KC + k, normed[k % 2])
            for j in range(7):
                split_hi(C0 + 2 + j)
                for k in range(4 * j + 4, 4 * j + 8):
                    if k < KC:
                        h_hi(k, 2 * KC + k, normed[k % 2])

            def hidden(j, bank, off=0):
                n = j + off
                if j >= 2:
                    act.wait_ge(dlo_done, n - 1)
                act.activation(relus[j % 2][:], ps[:, bank, :], ACT.Relu).then_inc(relu_done, 1)
                act.wait_ge(relu_done, n + 1)
                act.activation(squares[j % 2][:], relus[j % 2][:], ACT.Square).then_inc(dsq_done, 1)

            def hidden_hi(j, off=0):
                act.wait_ge(dsq_done, j + 1 + off)
                act.activation(ch(dhi, j % BLK), squares[j % 2][:], ACT.Copy).then_inc(dhi_done, 1)

            act.wait_ge(ada_used, ADA)
            act.wait_ge(unit_done, W2_0)
            for j in range(BLK):
                hidden(j, j)
                if j:
                    hidden_hi(j - 1)
                if j == 3:
                    split_hi(W2_0 + 1)
            hidden_hi(BLK - 1)
            with loop(ET.Activation, 0, NBLK - 1) as b:
                for m in range(BLK):
                    split_hi(W2_0 + m + 2, 16 * b)
                for j in range(BLK):
                    act.wait_ge(unit_done, 16 * b + (W2_0 + BLK + j + 1))
                    hidden(BLK + j, j % 2, 8 * b)
                    hidden_hi(BLK + j, 8 * b)
                    split_hi(W2_0 + BLK + j + 2, 16 * b)

            q = W2_0 + 16 * (NBLK - 1)
            for m in range(BLK):
                if m < BLK - 2:
                    split_hi(q + m + 2)
                if m == BLK - 2:
                    preload(ACT.Sqrt)
                for n in (2 * m, 2 * m + 1):
                    act.wait_ge(x2_done, 16 * (NBLK - 1) + n + 2)
                    if n >= 2:
                        act.wait_ge(ss2_done, n - 1)
                    act.activation((ta if n % 2 else sq)[:], ch(xb, n), ACT.Square).then_inc(x2sq_done, 1)
                    act.wait_ge(x2sq_done, n + 1)
                    act.activation(ch(xb, n), ch(xb, n), ACT.Copy, scale=col("final_g", n)).then_inc(fg_done, 1)
            root(4, 1)

        @block.vector
        def _(dve):
            steps = [0]

            def chain(ins):
                steps[0] += 1
                ins.then_inc(dv, 1)
                dve.wait_ge(dv, steps[0])

            dve.memset(ones[:], 1.0).then_inc(ones_set, 1)
            dve.memset(pacc[:, 0:1], 0.0).then_inc(conv_done, 1)
            dve.wait_ge(par_in, 16)
            dve.tensor_scalar(b1p[:, 0:KC], pr[:, COL["ada_b"]:COL["ada_b"] + 2 * KC:2], 1.0, None, ALU.add
                              ).then_inc(small, 1)
            dve.tensor_scalar(b1p[:, KC:2 * KC], col("ada_b", M_SC2, KC), 1.0, None, ALU.add).then_inc(small, 1)

            def variance(bank):
                chain(dve.tensor_scalar(st[:, 0:4], ps[:, bank, 0:4], 1.0 / D, EPS, ALU.mult, ALU.add))
                dve.reciprocal(st[:, 4:8], st[:, 0:4]).then_inc(var_done, 1)

            dve.wait_ge(xsq_used, KC)
            variance(6)
            dve.wait_ge(cs_ready, 1)

            def ada_reduce(a, off=0):
                wait_ada(dve, a, off)
                s = adar[:, a % 2, :]
                dve.scalar_tensor_tensor(s, s, 1.0, csb[:], ALU.mult, ALU.mult,
                                         accum_out=mod[:, bass.ds(a + off, 1)]).then_inc(ada_used, 1)

            def lo_part(k, n, src):
                dve.wait_ge(hhi_done, n + 1)
                dve.tensor_tensor(ch(hlo, k), src[:], f(ch(hhi, k)), ALU.subtract).then_inc(hlo_done, 1)

            def a0_chunk(k):
                first = isinstance(k, int)
                ada_reduce(0, 2 * k)
                if first:
                    dve.wait_ge(rstd_done, 1)
                else:
                    dve.wait_ge(hf_ready, k)
                dve.tensor_tensor(ta[:], ch(xb, k), rstd[:], ALU.mult).then_inc(dv, 1)
                ada_reduce(1, 2 * k)
                dve.wait_ge(ada_used, 2 * k + 1)
                dve.wait_ge(small, 2 * k + 2)
                dve.scalar_tensor_tensor(modb[:, bass.ds(2 * k, 1)], mod[:, bass.ds(2 * k, 1)],
                                         b1p[:, bass.ds(k, 1)], col("norm1_g", k), ALU.add, ALU.mult
                                         ).then_inc(small, 1)
                if not first:
                    lo_part(k - 1, k - 1, tb)
                dve.wait_ge(ada_used, 2 * k + 2)
                dve.tensor_tensor(modb[:, bass.ds(2 * k + 1, 1)], mod[:, bass.ds(2 * k + 1, 1)],
                                  col("ada_b", 2 * k + 1), ALU.add).then_inc(small, 1)
                if not first:
                    dve.wait_ge(hlo_done, k)
                dve.wait_ge(small, 2 * k + 4)
                dve.wait_ge(dv, k + (steps[0] + 1))
                dve.tensor_scalar(tb[:], ta[:], modb[:, bass.ds(2 * k, 1)], modb[:, bass.ds(2 * k + 1, 1)],
                                  ALU.mult, ALU.add).then_inc(hf_ready, 1)

            a0_chunk(0)
            with loop(ET.DVE, 1, KC) as k:
                a0_chunk(k)
            lo_part(KC - 1, KC - 1, tb)
            steps[0] += KC
            n_small = 2 + 2 * KC

            def glu(c, bank):
                dve.wait_ge(sig_done, c + 1)
                dve.scalar_tensor_tensor(ch(xb, c), ps[:, bank, :], col("b_in", c), sig[:], ALU.add, ALU.mult
                                         ).then_inc(glu_done, 1)

            def conv(c, bank, n0):
                acc0 = ps[:, bank, :]

                def tap(j):
                    return col("w_dw", c * TAPS + j)

                dve.wait_ge(glu_done, c + 1)
                dve.tensor_scalar(acc0, ch(xb, c), tap(30), col("b_dw", c), ALU.mult, ALU.add).then_inc(dv, 1)
                dve.wait_ge(conv_done, c + 1)
                dve.tensor_scalar(pacc[:, 1:T], ch(xb, c, 0, T - 1), tap(29), None, ALU.mult).then_inc(dv, 1)
                n = 2
                for j in range(28, -1, -1):
                    s = TAPS - 1 - j
                    acc = pacc[:, s:T] if j % 2 else acc0[:, s:T]
                    dve.wait_ge(dv, n0 + (n - 1))
                    dve.scalar_tensor_tensor(acc, ch(xb, c, 0, T - s), tap(j), acc, ALU.mult, ALU.add
                                             ).then_inc(dv, 1)
                    n += 1
                dve.wait_ge(dv, n0 + n)
                dve.tensor_tensor(ch(xb, c), acc0, pacc[:], ALU.add).then_inc(conv_done, 1)

            for c in range(4):
                glu(c, 2 * c)
            with loop(ET.DVE, 0, 6) as i:
                for s in range(2):
                    conv(2 * i + s, 4 + s, 2 * TAPS * i + (steps[0] + TAPS * s))
                    glu(2 * i + (4 + s), 2 * s)
            steps[0] += 12 * TAPS
            for c in range(12, KC):
                conv(c, 4 + c % 2, steps[0])
                steps[0] += TAPS

            dve.wait_ge(stat_done, 1)
            chain(dve.tensor_scalar(st[:, 12:16], ps[:, 0, 0:4], 1.0 / D, None, ALU.mult))
            chain(dve.tensor_tensor(st[:, 0:4], st[:, 12:16], st[:, 12:16], ALU.mult))
            chain(dve.scalar_tensor_tensor(st[:, 0:4], ps[:, 0, 4:8], 1.0 / D, st[:, 0:4], ALU.mult, ALU.subtract))
            chain(dve.tensor_scalar(st[:, 0:4], st[:, 0:4], 0.0, EPS, ALU.max, ALU.add))
            dve.reciprocal(st[:, 4:8], st[:, 0:4]).then_inc(var_done, 1)

            def z(k):
                if k < KC:
                    if k >= 2:
                        dve.wait_ge(hf_ready, KC + k - 1)
                    dve.tensor_tensor(scaled[k % 2][:], ch(xb, k), mu[:], ALU.subtract).then_inc(dv, 1)
                    steps[0] += 1
                if k >= 2:
                    lo_part(k - 2, KC + k - 2, silus[k % 2])
                if k < KC:
                    dve.wait_ge(dv, steps[0])
                    dve.tensor_tensor(normed[k % 2][:], scaled[k % 2][:], rstd[:], ALU.mult).then_inc(hf_ready, 1)

            def split_lo(q, off=0):
                dve.wait_ge(whi_done, q + 1 + off)
                dve.tensor_tensor(wlo[:, q % WS, :], raw[:, q % RAW, :], f(whi[:, q % WS, :]), ALU.subtract
                                  ).then_inc(wlo_done, 1)

            dve.wait_ge(rstd_done, 3)
            a = 2 * KC + ADA_A1
            for k in range(KC + 2):
                z(k)
                if k % 2:
                    ada_reduce(a)
                    a += 1
            while a < 2 * KC + ADA_A1 + ADA_B0:
                ada_reduce(a)
                a += 1
            dve.wait_ge(ada_used, M_SC2)
            dve.tensor_tensor(modb[:, M_G1:M_G1 + KC], mod[:, M_G1:M_G1 + KC], col("ada_b", M_G1, KC), ALU.add
                              ).then_inc(small, 1)
            dve.wait_ge(small, n_small + 1)
            dve.tensor_tensor(g1b[:], modb[:, M_G1:M_G1 + KC], col("b_out", 0, KC), ALU.mult).then_inc(small, 1)
            assert n_small + 2 == SMALL_G1

            def x1(n):
                dve.wait_ge(yg_done, n + 1)
                dve.wait_ge(xr_in[n // 4], 16)
                dve.tensor_tensor(ch(xb, n), sig[:], ch(xb, n), ALU.add).then_inc(x1_done, 1)

            def add_squares(n, done, seen, src=sq):
                dve.wait_ge(seen, n + 1)
                if n == 0:
                    dve.tensor_copy(ssum[:], src[:]).then_inc(done, 1)
                else:
                    dve.wait_ge(done, n)
                    dve.tensor_tensor(ssum[:], ssum[:], src[:], ALU.add).then_inc(done, 1)

            x1(0)
            x1(1)
            for n in range(2, 8):
                x1(n)
                add_squares(n - 2, ss1_done, x1sq_done)
            add_squares(6, ss1_done, x1sq_done)
            for j in range(8):
                for _ in range(ada_share(ADA_B1, j)):
                    ada_reduce(a)
                    a += 1
                x1(8 + j)
                add_squares(7 + j, ss1_done, x1sq_done)
            add_squares(15, ss1_done, x1sq_done)
            dve.wait_ge(ada_used, M_G2)
            dve.scalar_tensor_tensor(modb[:, M_SC2:M_SC2 + KC], mod[:, M_SC2:M_SC2 + KC], 1.0, b1p[:, KC:2 * KC],
                                     ALU.mult, ALU.add).then_inc(small, 1)
            dve.tensor_tensor(modb[:, M_SH2:M_SH2 + KC], mod[:, M_SH2:M_SH2 + KC], col("ada_b", M_SH2, KC), ALU.add
                              ).then_inc(small, 1)
            dve.wait_ge(small, SMALL_G1 + 2)
            dve.tensor_tensor(modb[:, M_SC2:M_SC2 + KC], modb[:, M_SC2:M_SC2 + KC], col("norm2_g", 0, KC), ALU.mult
                              ).then_inc(small, 1)
            dve.wait_ge(small, SMALL_G1 + 3)
            dve.wait_ge(stat_done, 2)
            variance(2)

            def h2(k):
                if k < KC:
                    if k >= 2:
                        dve.wait_ge(hf_ready, 2 * KC + k - 1)
                    dve.tensor_tensor(scaled[k % 2][:], ch(xb, k), rstd[:], ALU.mult).then_inc(dv, 1)
                    steps[0] += 1
                if k >= 2:
                    lo_part(k - 2, 2 * KC + k - 2, normed[k % 2])
                if k < KC:
                    dve.wait_ge(dv, steps[0])
                    if k >= 2:
                        dve.wait_ge(hlo_done, 2 * KC + k - 1)
                    dve.tensor_scalar(normed[k % 2][:], scaled[k % 2][:], modb[:, M_SC2 + k:M_SC2 + k + 1],
                                      modb[:, M_SH2 + k:M_SH2 + k + 1], ALU.mult, ALU.add).then_inc(hf_ready, 1)

            dve.wait_ge(rstd_done, 4)
            for k in range(KC + 2):
                h2(k)
                if k % 2 and a < ADA:
                    ada_reduce(a)
                    a += 1
            while a < ADA:
                ada_reduce(a)
                a += 1
            dve.wait_ge(ada_used, ADA)
            dve.tensor_tensor(modb[:, M_G2:M_G2 + KC], mod[:, M_G2:M_G2 + KC], col("ada_b", M_G2, KC), ALU.add
                              ).then_inc(x2_done, 1)

            def hidden_lo(j, off=0):
                dve.wait_ge(dhi_done, j + 1 + off)
                dve.tensor_tensor(ch(dlo, j % BLK), squares[j % 2][:], f(ch(dhi, j % BLK)), ALU.subtract).then_inc(dlo_done, 1)

            def x2(m, off=0):
                for nn in range(2):
                    n = 2 * m + nn
                    dve.scalar_tensor_tensor(ch(xb, n), ps[:, 4 + 2 * (m % 2) + nn, :],
                                             modb[:, M_G2 + n:M_G2 + n + 1], ch(xb, n), ALU.mult, ALU.add
                                             ).then_inc(x2_done, 1)

            for j in range(BLK):
                hidden_lo(j)
            dve.wait_ge(wlo_done, LO_POOL)
            with loop(ET.DVE, 0, NBLK - 1) as b:
                for m in range(BLK):
                    dve.wait_ge(unit_done, 16 * b + (W2_0 + m + 1))
                    if m == 0:
                        dve.wait_ge(x2_done, 16 * b + 1)
                    x2(m)
                    split_lo(W2_0 + m + 2, 16 * b)
                for j in range(BLK):
                    hidden_lo(BLK + j, 8 * b)
                    split_lo(W2_0 + BLK + j + 2, 16 * b)
            q = W2_0 + 16 * (NBLK - 1)
            for m in range(BLK):
                dve.wait_ge(unit_done, q + m + 1)
                if m == 0:
                    dve.wait_ge(x2_done, 16 * (NBLK - 1) + 1)
                x2(m)
                if m < BLK - 2:
                    split_lo(q + m + 2)
                add_squares(2 * m, ss2_done, x2sq_done, sq)
                add_squares(2 * m + 1, ss2_done, x2sq_done, ta)
            dve.wait_ge(stat_done, 3)
            variance(0)
            dve.wait_ge(fg_done, KC)
            dve.wait_ge(rstd_done, 5)
            for n in range(FIN_POOL):
                dve.tensor_tensor(ch(xb, n), ch(xb, n), ps[:, 1, :], ALU.mult).then_inc(fin_dve, 1)

        @block.gpsimd
        def _(pool):
            def split_lo(q, off=0):
                pool.wait_ge(whi_done, q + 1 + off)
                pool.tensor_tensor(wlo[:, q % WS, :], raw[:, q % RAW, :], f(whi[:, q % WS, :]), ALU.subtract
                                   ).then_inc(wlo_done, 1)

            def c_sums(c):
                pool.wait_ge(conv_done, c + 2)
                pool.wait_ge(s1_done, c + 1)
                pool.tensor_tensor(s1[:], s1[:], ch(xb, c), ALU.add).then_inc(s1_done, 1)
                pool.wait_ge(csq_done, c + 1)
                pool.wait_ge(s2_done, c + 1)
                pool.tensor_tensor(s2[:], s2[:], sq[:], ALU.add).then_inc(s2_done, 1)

            pool.memset(ident[:], 0.0).then_inc(ident_clear, 1)
            pool.wait_ge(ident_clear, 1)
            pool.affine_select(out=ident[:], in_=ident[:], compare_op=ALU.not_equal, fill=1.0, base=0,
                               pattern=[[-1, P]], channel_multiplier=1).then_inc(ident_set, 1)
            pool.memset(s1[:], 0.0).then_inc(s1_done, 1)
            pool.memset(s2[:], 0.0).then_inc(s2_done, 1)
            for q in range(A0, A1 + 2):
                split_lo(q)
            pool.wait_ge(ada_used, 2 * KC)
            pool.wait_ge(cs_ready, 1)
            with loop(ET.Pool, 0, 6) as i:
                for s in range(2):
                    split_lo(A1 + 2 + 2 * s, 4 * i)
                    split_lo(A1 + 3 + 2 * s, 4 * i)
                    wait_ada(pool, 2 * KC + s, 2 * i)
                    pool.tensor_tensor(adar[:, s, :], adar[:, s, :], csb[:], ALU.mult).then_inc(ada_mul, 1)
                    c_sums(2 * i + s)
            for c in range(12, KC):
                c_sums(c)
            for q in range(B0 + 2, LO_POOL):
                split_lo(q)
            pool.wait_ge(fg_done, KC)
            pool.wait_ge(rstd_done, 5)
            for n in range(FIN_POOL, KC):
                pool.tensor_tensor(ch(xb, n), ch(xb, n), rstd[:], ALU.mult).then_inc(fin_pool, 1)


def _tiles(m, rows, cols):
    t = m.reshape(m.shape[0] // P, P, m.shape[1] // P, P)[rows][:, :, cols]
    return t.transpose(1, 0, 2, 3).reshape(P, -1)


def _units(w_in, w_out, w1, w2):
    every = list(range(KC))
    in_cols = [h * KC + c for c in range(4) for h in range(2)]
    for j in range(8):
        yield _tiles(w_in, [2 * j, 2 * j + 1], in_cols)
    for c in range(4, KC):
        for h in range(2):
            yield _tiles(w_in, every, [h * KC + c])
    for j in range(8):
        yield _tiles(w_out, [2 * j, 2 * j + 1], list(range(8)))
    for j in range(8):
        yield _tiles(w_out, every, [8 + j])
    for b in range(NBLK):
        for j in range(BLK):
            if b == 0:
                yield _tiles(w1, [2 * j, 2 * j + 1], list(range(8)))
            else:
                yield _tiles(w1, every, [BLK * b + j])
        rows = list(range(BLK * b, BLK * (b + 1)))
        for m in range(BLK):
            yield np.concatenate([_tiles(w2, rows, [2 * m + nn]) for nn in range(2)], axis=1)


def kernel(x, c, ada_w, ada_b, norm1_g, norm2_g, mlp_w1, mlp_w2, final_g, conv_w_in, conv_b_in, conv_w_dw,
           conv_b_dw, conv_ln_g, conv_ln_b, conv_w_out, conv_b_out, **other_mixers):
    import concourse.bacc as bacc
    from concourse.bass_utils import run_bass_kernel_spmd

    def chunks(v):
        return np.asarray(v).reshape(-1, P).T

    order = [h * KC + k for k in range(KC) for h in (1, 0)]
    order += [part * KC + k for part in (2, 4, 3, 5) for k in range(KC)]
    w = np.stack(list(_units(np.asarray(conv_w_in)[0], np.asarray(conv_w_out)[0],
                             np.asarray(mlp_w1)[0], np.asarray(mlp_w2)[0])))
    ada = np.ascontiguousarray(np.asarray(ada_w)[0].T.reshape(ADA, P, D)[order])
    dw = np.asarray(conv_w_dw)[0].T.reshape(KC, P, TAPS).transpose(1, 0, 2).reshape(P, -1)
    packed = {"ada_b": chunks(np.asarray(ada_b)[0])[:, order], "norm1_g": chunks(norm1_g), "norm2_g": chunks(norm2_g),
              "final_g": chunks(final_g), "b_in": chunks(conv_b_in), "b_dw": chunks(conv_b_dw),
              "ln_g": chunks(conv_ln_g), "ln_b": chunks(conv_ln_b), "b_out": chunks(conv_b_out), "w_dw": dw}
    arrays = {
        "xT": np.ascontiguousarray(np.asarray(x)[0].T),
        "c": np.ascontiguousarray(np.asarray(c)[0]),
        "w": w,
        "ada": ada,
        "par": np.ascontiguousarray(np.concatenate([packed[name] for name, _ in PARAMS], axis=1)),
    }
    nc = bacc.Bacc("TRN2", target_bir_lowering=False, num_devices=1)
    aps = {n: nc.dram_tensor(n, a.shape, F32, kind="ExternalInput").ap() for n, a in arrays.items()}
    out = nc.dram_tensor("out", (D, T), F32, kind="ExternalOutput").ap()
    trunk_kernel(nc, aps["xT"], aps["c"], aps["w"].rearrange("q p n -> p q n"),
                 aps["ada"].rearrange("a p n -> p a n"), aps["par"], out)
    r = run_bass_kernel_spmd(nc, [arrays], core_ids=[0])
    return np.ascontiguousarray(r.results[0]["out"].T).reshape(1, T, D)
```

```python
from contextlib import ExitStack

import numpy as np

import concourse.bass as bass
from concourse import mybir

F32 = mybir.dt.float32
F32R = mybir.dt.float32r
ALU = mybir.AluOpType
ACT = mybir.ActivationFunctionType
ET = mybir.EngineType

P = 128
D = 2048
T = 512
KC = D // P
FF = 4 * D
BLK = 8
NBLK = FF // P // BLK
TAPS = 31
SIDE = (28, 27, 26, 25)
CHAIN = 26
PE_TAPS = 12
EPS = 1e-6
TILES = 16
U = TILES * P
RAW = 4
WS = 2

A0, A1, B0, B1, C0, W2_0 = 0, 8, 32, 40, 48, 56
NUNITS = C0 + 2 * BLK * NBLK
LO_POOL = W2_0 + 2

M_G1, M_SC2, M_SH2, M_G2 = 2 * KC, 3 * KC, 4 * KC, 5 * KC
ADA = 6 * KC
ADA_A1, ADA_B0, ADA_B1, ADA_C0 = 12, 17, 17, 18

SH2_EARLY = KC + 2 * KC + ADA_A1 + ADA_B0 + ADA_B1 - M_G2
HIDDEN_ORDER = (4, 5, 0, 1, 2, 3, 6, 7)
LATE = 14
FIN_POOL = 11
SMALL_G1 = 2 * KC + 4

PARAMS = [("ada_b", ADA), ("norm1_g", KC), ("norm2_g", KC), ("final_g", KC), ("b_in", 2 * KC), ("b_dw", KC),
          ("ln_g", KC), ("ln_b", KC), ("b_out", KC), ("w_dw", KC * TAPS)]
COL, _n = {}, 0
for _name, _w in PARAMS:
    COL[_name] = _n
    _n += _w
NPAR = _n


def trunk_kernel(nc, xT, c, w, ada, par, out):
    x_d = xT.rearrange("(k p) t -> p k t", p=P)
    out_d = out.rearrange("(k p) t -> p k t", p=P)

    with ExitStack() as ctx:
        def sb(name, shape, dt=F32, scope=ctx):
            return scope.enter_context(nc.sbuf_tensor(name, shape, dt))

        def sem(name):
            return ctx.enter_context(nc.semaphore(name))

        with ExitStack() as between:
            diags = sb("diags", [P, 2 * PE_TAPS * P], scope=between)
        hhi = sb("hhi", [P, KC * T], F32R)
        xb = sb("xb", [P, KC * T])
        hlo = sb("hlo", [P, KC * T], F32R)
        raw = sb("raw", [P, RAW, U])
        whi = sb("whi", [P, WS, U], F32R)
        wlo = sb("wlo", [P, WS, U], F32R)
        pr = sb("pr", [P, NPAR])
        mod = sb("mod", [P, ADA])
        modb = sb("modb", [P, ADA])
        b1p = sb("b1p", [P, 2 * KC])
        g1b = sb("g1b", [P, KC])
        rstd = sb("rstd", [P, T])
        ta = sb("ta", [P, T])
        tb = sb("tb", [P, T])
        sq = sb("sq", [P, T])
        ssum = sb("ssum", [P, T])
        st = sb("st", [P, 16])
        ones = sb("ones", [P, 1])
        ident = sb("ident", [P, P])
        dump = sb("dump", [P, 1])
        with ExitStack() as early:
            csb = sb("csb", [P, D], scope=early)
            adar = sb("adar", [P, 2, D], scope=early)
            sig = sb("sig", [P, T], scope=early)
            pacc = sb("pacc", [P, T], scope=early)
            s1 = sb("s1", [P, T], scope=early)
            s2 = sb("s2", [P, T], scope=early)
        dhi = sb("dhi", [P, BLK * T], F32R)
        dlo = sb("dlo", [P, BLK * T], F32R)
        ps = ctx.enter_context(nc.psum_tensor("ps", [P, 8, T], F32))
        mu = ssum
        scaled, normed, silus = (ta, s1), (tb, s2), (sq, pacc)
        relus, squares = (ta, tb), (sq, ssum)
        first_squares = (ta, tb, sq, ssum)

        def f(ap):
            return ap.bitcast(F32)

        def ch(buf, k, lo=0, n=T):
            return buf[:, bass.ds(k * T + lo, n)]

        def col(name, k, n=1):
            return pr[:, bass.ds(COL[name] + k, n)]

        x_in = [sem(f"x_in{i}") for i in range(4)]
        xr_in = [sem(f"xr_in{i}") for i in range(4)]
        c_in, par_in = sem("c_in"), sem("par_in")
        raw_in = [sem(f"raw_in{i}") for i in range(RAW)]
        ada_in = [sem(f"ada_in{i}") for i in range(2)]
        out_done = sem("out_done")
        ones_set, ident_clear, ident_set = sem("ones_set"), sem("ident_clear"), sem("ident_set")
        cs_ready = sem("cs_ready")
        whi_done = sem("whi_done")
        wlo_done = sem("wlo_done")
        unit_done = sem("unit_done")
        ada_mul = sem("ada_mul")
        ada_used = sem("ada_used")
        small = sem("small")
        xsq_done = sem("xsq_done")
        xsq_used = sem("xsq_used")
        stat_done = sem("stat_done")
        var_done = sem("var_done")
        root_done = sem("root_done")
        spread_done = sem("spread_done")
        rstd_done = sem("rstd_done")
        warm = sem("warm")
        dv = sem("dv")
        ac = sem("ac")
        hf_ready = sem("hf_ready")
        hhi_done = sem("hhi_done")
        hlo_done = sem("hlo_done")
        sig_done = sem("sig_done")
        tb_clear = sem("tb_clear")
        side_mul = sem("side_mul")
        side_add = sem("side_add")
        acc_set = sem("acc_set")
        diag_done = sem("diag_done")
        pe_taps_done = sem("pe_taps_done")
        ln_used = sem("ln_used")
        glu_done = sem("glu_done")
        conv_done = sem("conv_done")
        csq_done = sem("csq_done")
        s1_done = sem("s1_done")
        s2_done = sem("s2_done")
        yg_done = sem("yg_done")
        x1_done = sem("x1_done")
        x1sq_done = sem("x1sq_done")
        ss1_done = sem("ss1_done")
        relu_done = sem("relu_done")
        dsq_done = sem("dsq_done")
        dhi_done = sem("dhi_done")
        dlo_done = sem("dlo_done")
        x2_done = sem("x2_done")
        x2sq_done = sem("x2sq_done")
        ss2_done = sem("ss2_done")
        fg_done = sem("fg_done")
        fin_dve = sem("fin_dve")
        fin_pool = sem("fin_pool")

        block = ctx.enter_context(nc.Block())

        def loop(eng, n0, n1):
            return nc.Fori(n0, n1, engines=(eng,))

        def ada_share(n, j):
            return (j + 1) * n // 8 - j * n // 8

        def wait_raw(eng, q, off=0):
            eng.wait_ge(raw_in[q % RAW], 16 * (q // RAW + 1) + (16 // RAW) * off)

        def wait_ada(eng, a, off=0):
            eng.wait_ge(ada_in[a % 2], 16 * (a // 2 + 1) + 8 * off)

        @block.sync
        def _(sp):
            sp.dma_start(csb[:], c.partition_broadcast(P)).then_inc(c_in, 16)
            sp.dma_start(pr[:], par).then_inc(par_in, 16)
            def load_unit(q, off=0):
                if q >= RAW:
                    sp.wait_ge(wlo_done, q - RAW + 1 + off)
                sp.dma_start(raw[:, q % RAW:q % RAW + 1, :], w[:, bass.ds(q + off, 1), :]
                             ).then_inc(raw_in[q % RAW], 16)

            def load_ada(a, off=0):
                if a >= 2:
                    sp.wait_ge(ada_used, a - 1 + off)
                sp.dma_start(adar[:, a % 2:a % 2 + 1, :], ada[:, bass.ds(a + off, 1), :]
                             ).then_inc(ada_in[a % 2], 16)

            load_ada(0)
            load_ada(1)
            for i in range(4):
                sp.dma_start(xb[:, 4 * i * T:4 * (i + 1) * T].rearrange("p (k t) -> p k t", t=T),
                             x_d[:, 4 * i:4 * i + 4, :]).then_inc(x_in[i], 16)
            load_ada(2)
            load_ada(3)
            load_unit(0)
            load_unit(1)
            for q in range(2, A1 + 1):
                for a in range(4 * q - 4, 4 * q):
                    load_ada(a)
                if q < A1:
                    load_unit(q)
            a = 2 * KC
            load_unit(A1)
            load_unit(A1 + 1)
            with loop(ET.SP, 0, 6) as i:
                for s in range(2):
                    load_unit(A1 + 2 + 2 * s, 4 * i)
                    load_unit(A1 + 3 + 2 * s, 4 * i)
                    load_ada(2 * KC + s, 2 * i)
            a += ADA_A1

            def x_again(g):
                sp.wait_ge(hf_ready, KC + 4 * g + 4)
                sp.dma_start(xb[:, 4 * g * T:4 * (g + 1) * T].rearrange("p (k t) -> p k t", t=T),
                             x_d[:, 4 * g:4 * g + 4, :]).then_inc(xr_in[g], 16)

            for q0, n_ada in ((B0, ADA_B0), (B1, ADA_B1), (C0, ADA_C0)):
                for j in range(8):
                    load_unit(q0 + 2 + j)
                    for _ in range(ada_share(n_ada, j)):
                        load_ada(a)
                        a += 1
                    if q0 == B0 and j % 2 and j > 1:
                        x_again(j // 2 - 1)
                if q0 == B0:
                    x_again(3)
            assert a == ADA
            load_unit(W2_0 + 2)
            load_unit(W2_0 + 3)
            with loop(ET.SP, 1, (NUNITS - W2_0) // RAW) as i:
                for q in range(RAW):
                    load_unit(W2_0 + q, 4 * i)
            stores = [(fin_dve, n, min(2, FIN_POOL - n)) for n in range(0, FIN_POOL, 2)]
            for i, n in enumerate(range(FIN_POOL, KC)):
                stores.insert(2 * i + 1, (fin_pool, n, 1))
            for done, n, m in stores:
                sp.wait_ge(done, n + m - (FIN_POOL if done is fin_pool else 0))
                sp.dma_start(out_d[:, n:n + m, :], xb[:, n * T:(n + m) * T].rearrange("p (k t) -> p k t", t=T)
                             ).then_inc(out_done, 16)
            sp.wait_ge(out_done, 16 * len(stores))

        @block.tensor
        def _(pe):
            def product(bank, slot, tile, xhi, xlo, first, last):
                t = slice(tile * P, (tile + 1) * P)
                out = ps[:, bank, :]
                pe.matmul(out, whi[:, slot, t], xhi, start=first, stop=False, skip_group_check=True)
                pe.matmul(out, whi[:, slot, t], xlo, start=False, stop=False, skip_group_check=True)
                return pe.matmul(out, wlo[:, slot, t], xhi, start=False, stop=last, skip_group_check=True)

            def outer_unit(q, s, h0, i=None):
                i, first = (0, s == 0) if i is None else (i, False)
                pe.wait_ge(wlo_done, 2 * i + (q + s + 1))
                for kk in range(2):
                    k = 4 * i + (2 * s + kk)
                    pe.wait_ge(hlo_done, k + (h0 + 1))
                    for o in range(8):
                        last = product(o, s, 8 * kk + o, ch(hhi, k), ch(hlo, k), first and kk == 0, False)
                last.then_inc(unit_done, 1)

            def outer_units(q, h0):
                for s in range(2):
                    outer_unit(q, s, h0)
                with loop(ET.PE, 1, 4) as i:
                    for s in range(2):
                        outer_unit(q, s, h0, i)

            def inner_unit(slot, bank, seen):
                pe.wait_ge(wlo_done, seen)
                for k in range(KC):
                    last = product(bank, slot, k, ch(hhi, k), ch(hlo, k), k == 0, k == KC - 1)
                last.then_inc(unit_done, 1)

            def token_sums(bank, col0, src, start):
                for j in range(T // P):
                    last = pe.matmul(ps[:, bank, col0 + j:col0 + j + 1], src[:, j * P:(j + 1) * P], ones[:],
                                     start=start and j == 0, stop=False, skip_group_check=True)
                return last

            def spread(bank, col0):
                for j in range(T // P):
                    last = pe.matmul(ps[:, bank, j * P:(j + 1) * P], st[:, col0 + j:col0 + j + 1].to_broadcast([P, P]),
                                     ident[:], start=j == 0, stop=False, skip_group_check=True)
                last.then_inc(spread_done, 1)

            pe.wait_ge(ones_set, 1)
            pe.wait_ge(xsq_used, KC)
            token_sums(6, 0, ssum, True).then_inc(stat_done, 1)
            pe.wait_ge(ident_set, 1)
            pe.wait_ge(root_done, 1)
            spread(7, 8)
            pe.wait_ge(rstd_done, 1)
            outer_units(A0, 0)
            with loop(ET.PE, 0, 6) as i:
                for s in range(2):
                    pe.wait_ge(glu_done, 2 * i + (3 + s))
                    inner_unit(0, 2 * s, 4 * i + (A1 + 2 * s + 1))
                    inner_unit(1, 2 * s + 1, 4 * i + (A1 + 2 * s + 2))
            for n, c in enumerate((KC - 2, KC - 1)):
                pe.wait_ge(glu_done, c + 1)
                for j in range(PE_TAPS - 1, -1, -1):
                    back, d = TAPS - 1 - j, n * PE_TAPS + j
                    pe.wait_ge(diag_done, n * PE_TAPS + PE_TAPS - j)
                    last = pe.matmul(ps[:, 1 + 2 * n, back:T], diags[:, d * P:(d + 1) * P], ch(xb, c, 0, T - back),
                                     start=j == PE_TAPS - 1, stop=False, skip_group_check=True)
                last.then_inc(pe_taps_done, 1)
            pe.wait_ge(s1_done, LATE + 1)
            token_sums(0, 0, s1, True)
            pe.wait_ge(s2_done, LATE + 1)
            token_sums(0, 4, s2, False)
            for c in range(LATE, KC):
                pe.wait_ge(conv_done, c + 2)
                token_sums(0, 0, ch(xb, c), False)
                pe.wait_ge(csq_done, c + 1)
                token_sums(0, 4, sig if c % 2 else sq, False).then_inc(ln_used, 1)
            pe.wait_ge(root_done, 2)
            spread(1, 8)
            spread(2, 12)
            outer_units(B0, KC)
            for s in range(2):
                pe.wait_ge(yg_done, s + 1)
                inner_unit(s, s, B1 + s + 1)
            with loop(ET.PE, 1, 4) as i:
                for s in range(2):
                    pe.wait_ge(yg_done, 2 * i + (7 + s))
                    inner_unit(s, s, 2 * i + (B1 + s + 1))
            pe.wait_ge(ss1_done, KC)
            token_sums(2, 0, ssum, True).then_inc(stat_done, 1)
            pe.wait_ge(root_done, 3)
            spread(3, 8)
            outer_units(C0, 2 * KC)

            def w2_unit(m, seen, wait_hidden=None):
                pe.wait_ge(wlo_done, seen)
                for nn in range(2):
                    for k in range(BLK):
                        if wait_hidden is not None and nn == 0:
                            pe.wait_ge(dlo_done, wait_hidden + (k + 1))
                        last = product(4 + 2 * (m % 2) + nn, m % 2, 8 * nn + k, ch(dhi, k), ch(dlo, k),
                                       k == 0, k == BLK - 1)
                last.then_inc(unit_done, 1)

            def w2_rest(b):
                w2_unit(1, 16 * b + (W2_0 + 2))
                with loop(ET.PE, 1, 4) as i:
                    for s in range(2):
                        pe.wait_ge(x2_done, 16 * b + 4 * i + (2 * s - 1))
                        w2_unit(s, 16 * b + 2 * i + (W2_0 + s + 1))

            pe.wait_ge(wlo_done, W2_0 + 1)
            pe.wait_ge(relu_done, 2)
            for n, k in enumerate(HIDDEN_ORDER):
                pe.wait_ge(dlo_done, n + 1)
                for nn in range(2):
                    last = product(4 + nn, 0, 8 * nn + k, ch(dhi, k), ch(dlo, k), n == 0, n == BLK - 1)
            last.then_inc(unit_done, 1)
            pe.wait_ge(relu_done, BLK)
            with loop(ET.PE, 0, NBLK - 1) as b:
                w2_rest(b)
                with loop(ET.PE, 0, 4) as i:
                    for s in range(2):
                        pe.wait_ge(relu_done, 8 * b + 2 * i + (BLK + s - 1))
                        inner_unit(s, s, 16 * b + 2 * i + (W2_0 + BLK + s + 1))
                pe.wait_ge(x2_done, 16 * b + 17)
                w2_unit(0, 16 * b + (W2_0 + 2 * BLK + 1), 8 * b + BLK)
            w2_rest(NBLK - 1)
            pe.wait_ge(ss2_done, KC)
            token_sums(0, 0, ssum, True).then_inc(stat_done, 1)
            pe.wait_ge(root_done, 4)
            spread(1, 8)

        @block.scalar
        def _(act):
            def split_hi(q, off=0):
                wait_raw(act, q, off)
                if q >= WS:
                    act.wait_ge(unit_done, q - WS + 1 + off)
                act.activation(whi[:, q % WS, :], raw[:, q % RAW, :], ACT.Copy).then_inc(whi_done, 1)

            def preload(func):
                act.wait_ge(ones_set, 1)
                act.activation(dump[:], ones[:], func).then_inc(warm, 1)

            def root(n, bank, mean_bank=None):
                act.wait_ge(var_done, n)
                act.activation(st[:, 8:12], st[:, 4:8], ACT.Sqrt).then_inc(root_done, 1)
                if mean_bank is not None:
                    preload(ACT.Silu)
                act.wait_ge(spread_done, n + (n > 2))
                act.activation(rstd[:], ps[:, bank, :], ACT.Copy).then_inc(rstd_done, 1)
                if mean_bank is not None:
                    act.wait_ge(spread_done, n + 1)
                    act.activation(mu[:], ps[:, mean_bank, :], ACT.Copy).then_inc(rstd_done, 1)

            def h_hi(k, n, src):
                act.wait_ge(hf_ready, n + 1)
                act.activation(ch(hhi, k), src[:], ACT.Copy).then_inc(hhi_done, 1)

            act.wait_ge(c_in, 16)
            act.activation(csb[:], csb[:], ACT.Silu).then_inc(cs_ready, 1)
            preload(ACT.Sqrt)
            for k in range(KC):
                act.wait_ge(x_in[k // 4], 16)
                if k >= 2:
                    act.wait_ge(xsq_used, k - 1)
                act.activation((sq if k % 2 else sig)[:], ch(xb, k), ACT.Square).then_inc(xsq_done, 1)
            root(1, 7)
            preload(ACT.Sigmoid)
            for j in range(8):
                h_hi(2 * j, 2 * j, tb)
                split_hi(j)
                h_hi(2 * j + 1, 2 * j + 1, tb)

            act.wait_ge(par_in, 16)

            def sigmoid(c, bank, n):
                act.wait_ge(glu_done, n)
                act.activation(sig[:], ps[:, bank, :], ACT.Sigmoid, bias=col("b_in", c + KC)).then_inc(sig_done, 1)

            def c_square(c):
                act.wait_ge(conv_done, c + 2)
                late = isinstance(c, int) and c > LATE
                if not late:
                    act.wait_ge(s2_done, c + 1)
                act.activation((sig if late and c % 2 else sq)[:], ch(xb, c), ACT.Square).then_inc(csq_done, 1)

            def side_products(c):
                act.wait_ge(glu_done, c + 1)
                if not (isinstance(c, int) and c == 0):
                    act.wait_ge(acc_set, 2 * c)
                for out, j in zip((pacc, ta, ssum, rstd), SIDE):
                    last = act.activation(out[:, TAPS - 1 - j:T], ch(xb, c, 0, T - (TAPS - 1 - j)), ACT.Copy,
                                          scale=col("w_dw", c * TAPS + j))
                last.then_inc(side_mul, 1)

            def begin_sums(c, s):
                if not isinstance(c, int) or c >= 2:
                    act.wait_ge(conv_done, c)
                act.activation(ps[:, 4 + s, :], ch(xb, c), ACT.Identity, scale=col("w_dw", c * TAPS + 30),
                               bias=col("b_dw", c)).then_inc(acc_set, 1)
                act.wait_ge(side_add, 3 * c + 3)
                act.activation(ps[:, 6 + s, :], pacc[:], ACT.Copy).then_inc(acc_set, 1)

            split_hi(8)
            act.wait_ge(unit_done, A1)
            for c in range(4):
                sigmoid(c, 2 * c + 1, c)
                if c == 0:
                    split_hi(9)
            side_products(0)
            act.wait_ge(glu_done, 4)
            begin_sums(0, 0)
            side_products(1)
            begin_sums(1, 1)

            def ada_sum(a, off):
                act.wait_ge(ada_mul, a - 2 * KC + 1 + off)
                act.activation(adar[:, a % 2, :], adar[:, a % 2, :], ACT.Copy,
                               accum_out=mod[:, bass.ds(a + off, 1)]).then_inc(ada_used, 1)

            def a1_chunk(i, s):
                first = isinstance(i, int) and i == 0 and s == 0
                split_hi(A1 + 2 + 2 * s, 4 * i)
                if not first:
                    ada_sum(2 * KC + s - 1, 2 * i)
                    c_square(2 * i + (s - 1))
                split_hi(A1 + 3 + 2 * s, 4 * i)
                sigmoid(2 * i + (4 + s), 2 * s + 1, 2 * i + (4 + s))
                side_products(2 * i + (2 + s))
                begin_sums(2 * i + (2 + s), s)

            def diagonals(n):
                for j in range(PE_TAPS - 1, -1, -1):
                    d = n * PE_TAPS + j
                    act.activation(diags[:, d * P:(d + 1) * P], ident[:], ACT.Copy,
                                   scale=col("w_dw", (KC - 2 + n) * TAPS + j)).then_inc(diag_done, 1)

            a1_chunk(0, 0)
            a1_chunk(0, 1)
            with loop(ET.Activation, 1, 4) as i:
                a1_chunk(i, 0)
                a1_chunk(i, 1)
            for c in range(12, KC):
                q = A1 + 2 * (c - 4)
                split_hi(q + 2)
                ada_sum(2 * KC + c - 5, 0)
                c_square(c - 5)
                if c == 12 or c == KC - 1:
                    n = 10 if c == 12 else 14
                    side_products(n)
                    begin_sums(n, 0)
                split_hi(q + 3)
                sigmoid(c, 2 * (c % 2) + 1, c)
                if c < KC - 1:
                    side_products(c - 1)
                    begin_sums(c - 1, (c - 1) % 2)
            act.wait_ge(ident_set, 1)
            diagonals(0)
            side_products(KC - 1)
            diagonals(1)
            preload(ACT.Sqrt)
            begin_sums(KC - 1, 1)
            for c in range(11, KC):
                c_square(c)
            root(2, 1, 2)

            def z(k):
                if k < KC:
                    act.wait_ge(hf_ready, KC + k + 1)
                    if k >= 2:
                        act.wait_ge(hlo_done, KC + k - 1)
                    act.activation(silus[k % 2][:], normed[k % 2][:], ACT.Silu, scale=col("ln_g", k),
                                   bias=col("ln_b", k)).then_inc(ac, 1)
                if k:
                    act.wait_ge(ac, k)
                    act.activation(ch(hhi, k - 1), silus[(k - 1) % 2][:], ACT.Copy).then_inc(hhi_done, 1)

            for k in range(6):
                z(k)
            for j in range(7):
                split_hi(B0 + 2 + j)
                for k in range(4 * j + 6, 4 * j + 10):
                    if k <= KC:
                        z(k)

            def gated(n, bank):
                if n:
                    act.wait_ge(x1_done, n)
                act.activation(sig[:], ps[:, bank, :], ACT.Identity, scale=modb[:, M_G1 + n:M_G1 + n + 1],
                               bias=g1b[:, n:n + 1]).then_inc(yg_done, 1)

            def x1_square(n):
                act.wait_ge(x1_done, n + 1)
                if n:
                    act.wait_ge(ss1_done, n)
                act.activation(sq[:], ch(xb, n), ACT.Square).then_inc(x1sq_done, 1)

            act.wait_ge(small, SMALL_G1)
            act.wait_ge(unit_done, B1)
            gated(0, 0)
            gated(1, 1)
            split_hi(B1 + 1)
            for n in range(2, 8):
                gated(n, n)
                x1_square(n - 2)
            x1_square(6)
            for j in range(8):
                n = 8 + j
                x1_square(n - 1)
                if j == 7:
                    preload(ACT.Sqrt)
                act.wait_ge(unit_done, B1 + j + 1)
                gated(n, j % 2)
                if j < 7:
                    split_hi(B1 + j + 2)
            x1_square(15)
            split_hi(C0 + 1)
            root(3, 3)
            for k in range(6):
                h_hi(k, 2 * KC + k, normed[k % 2])
            for j in range(7):
                split_hi(C0 + 2 + j)
                for k in range(4 * j + 6, 4 * j + 10):
                    if k < KC:
                        h_hi(k, 2 * KC + k, normed[k % 2])

            def hidden(j, bank, off=0):
                n = j + off
                act.wait_ge(dlo_done, n - 1)
                act.activation(relus[j % 2][:], ps[:, bank, :], ACT.Relu).then_inc(relu_done, 1)
                act.wait_ge(relu_done, n + 1)
                act.activation(squares[j % 2][:], relus[j % 2][:], ACT.Square).then_inc(dsq_done, 1)

            def hidden_hi(j, off=0):
                act.wait_ge(dsq_done, j + 1 + off)
                act.activation(ch(dhi, j % BLK), squares[j % 2][:], ACT.Copy).then_inc(dhi_done, 1)

            act.wait_ge(unit_done, W2_0)
            for n in range(BLK + 1):
                if n < BLK:
                    if n >= 4:
                        act.wait_ge(dlo_done, n - 3)
                    act.activation(first_squares[n % 4][:], ps[:, HIDDEN_ORDER[n], :], ACT.Relu
                                   ).then_inc(relu_done, 1)
                if n == 1:
                    act.wait_ge(ada_used, ADA)
                if n:
                    act.wait_ge(dsq_done, n)
                    act.activation(ch(dhi, HIDDEN_ORDER[n - 1]), first_squares[(n - 1) % 4][:], ACT.Copy
                                   ).then_inc(dhi_done, 1)
                if n == 4:
                    split_hi(W2_0 + 1)
            with loop(ET.Activation, 0, NBLK - 1) as b:
                for m in range(BLK):
                    split_hi(W2_0 + m + 2, 16 * b)
                for j in range(BLK):
                    act.wait_ge(unit_done, 16 * b + (W2_0 + BLK + j + 1))
                    hidden(BLK + j, j % 2, 8 * b)
                    hidden_hi(BLK + j, 8 * b)
                    split_hi(W2_0 + BLK + j + 2, 16 * b)

            q = W2_0 + 16 * (NBLK - 1)
            for m in range(BLK):
                if m < BLK - 2:
                    split_hi(q + m + 2)
                if m == BLK - 2:
                    preload(ACT.Sqrt)
                for n in (2 * m, 2 * m + 1):
                    act.wait_ge(x2_done, 16 * (NBLK - 1) + n + 2)
                    if n >= 2:
                        act.wait_ge(ss2_done, n - 1)
                    act.activation((ta if n % 2 else sq)[:], ch(xb, n), ACT.Square).then_inc(x2sq_done, 1)
                    act.wait_ge(x2sq_done, n + 1)
                    act.activation(ch(xb, n), ch(xb, n), ACT.Copy, scale=col("final_g", n)).then_inc(fg_done, 1)
            root(4, 1)

        @block.vector
        def _(dve):
            steps = [0]

            def chain(ins):
                steps[0] += 1
                ins.then_inc(dv, 1)
                dve.wait_ge(dv, steps[0])

            dve.memset(ones[:], 1.0).then_inc(ones_set, 1)
            dve.memset(pacc[:, 0:2], 0.0).then_inc(conv_done, 1)
            dve.wait_ge(par_in, 16)
            dve.tensor_scalar(b1p[:, 0:KC], pr[:, COL["ada_b"]:COL["ada_b"] + 2 * KC:2], 1.0, None, ALU.add
                              ).then_inc(small, 1)
            dve.tensor_scalar(b1p[:, KC:2 * KC], col("ada_b", M_SC2, KC), 1.0, None, ALU.add).then_inc(small, 1)

            def variance(bank):
                chain(dve.tensor_scalar(st[:, 0:4], ps[:, bank, 0:4], 1.0 / D, EPS, ALU.mult, ALU.add))
                dve.reciprocal(st[:, 4:8], st[:, 0:4]).then_inc(var_done, 1)

            def ada_reduce(a, off=0):
                wait_ada(dve, a, off)
                s = adar[:, a % 2, :]
                dve.scalar_tensor_tensor(s, s, 1.0, csb[:], ALU.mult, ALU.mult,
                                         accum_out=mod[:, bass.ds(a + off, 1)]).then_inc(ada_used, 1)

            def lo_part(k, n, src):
                dve.wait_ge(hhi_done, n + 1)
                dve.tensor_tensor(ch(hlo, k), src[:], f(ch(hhi, k)), ALU.subtract).then_inc(hlo_done, 1)

            def a0_chunk(k, more=True):
                first = isinstance(k, int) and k == 0
                if more:
                    ada_reduce(0, 2 * k + 2)
                dve.wait_ge(small, 2 * k + 2)
                dve.scalar_tensor_tensor(modb[:, bass.ds(2 * k, 1)], mod[:, bass.ds(2 * k, 1)],
                                         b1p[:, bass.ds(k, 1)], col("norm1_g", k), ALU.add, ALU.mult
                                         ).then_inc(small, 1)
                dve.tensor_tensor(modb[:, bass.ds(2 * k + 1, 1)], mod[:, bass.ds(2 * k + 1, 1)],
                                  col("ada_b", 2 * k + 1), ALU.add).then_inc(small, 1)
                if more and not first:
                    ada_reduce(1, 2 * k + 2)
                if first:
                    dve.wait_ge(rstd_done, 1)
                else:
                    dve.wait_ge(hf_ready, k)
                dve.tensor_tensor(ta[:], ch(xb, k), rstd[:], ALU.mult).then_inc(dv, 1)
                if not first:
                    lo_part(k - 1, k - 1, tb)
                    dve.wait_ge(hlo_done, k)
                dve.wait_ge(small, 2 * k + 4)
                dve.wait_ge(dv, k + (steps[0] + 1))
                dve.tensor_scalar(tb[:], ta[:], modb[:, bass.ds(2 * k, 1)], modb[:, bass.ds(2 * k + 1, 1)],
                                  ALU.mult, ALU.add).then_inc(hf_ready, 1)
                if first:
                    ada_reduce(1, 2)
                if more:
                    dve.wait_ge(ada_used, 2 * k + 4)

            def add_squares(n, done, seen, src=sq):
                dve.wait_ge(seen, n + 1)
                if n == 0:
                    dve.tensor_copy(ssum[:], src[:]).then_inc(done, 1)
                else:
                    dve.wait_ge(done, n)
                    dve.tensor_tensor(ssum[:], ssum[:], src[:], ALU.add).then_inc(done, 1)

            dve.wait_ge(cs_ready, 1)
            ada_reduce(0)
            ada_reduce(1)
            for k in range(KC):
                add_squares(k, xsq_used, xsq_done, sq if k % 2 else sig)
            dve.wait_ge(stat_done, 1)
            variance(6)
            dve.wait_ge(ada_used, 2)
            a0_chunk(0)
            with loop(ET.DVE, 1, KC - 1) as k:
                a0_chunk(k)
            a0_chunk(KC - 1, more=False)
            lo_part(KC - 1, KC - 1, tb)
            dve.wait_ge(hlo_done, KC)
            dve.memset(tb[:, 0:1], 0.0).then_inc(tb_clear, 1)
            steps[0] += KC
            n_small = 2 + 2 * KC

            def glu(c, bank):
                dve.wait_ge(sig_done, c + 1)
                dve.scalar_tensor_tensor(ch(xb, c), ps[:, bank, :], col("b_in", c), sig[:], ALU.add, ALU.mult
                                         ).then_inc(glu_done, 1)

            def conv(c, s, n0):
                acc = ps[:, 4 + s, :], ps[:, 6 + s, :]
                shared = isinstance(c, int) and c >= KC - 2
                taps = list(range(24, PE_TAPS - 1 if shared else -1, -1)) + [29]
                for n, j in enumerate(taps):
                    back = TAPS - 1 - j
                    if n < 2:
                        dve.wait_ge(acc_set, 2 * c + 2)
                    else:
                        dve.wait_ge(dv, n0 + (n - 1))
                    out = acc[n % 2]
                    if j == 29:
                        assert n % 2 == 1
                        dve.wait_ge(conv_done, c + 1)
                        out = tb
                    dve.scalar_tensor_tensor(out[:, back:T], ch(xb, c, 0, T - back), col("w_dw", c * TAPS + j),
                                             acc[n % 2][:, back:T], ALU.mult, ALU.add).then_inc(dv, 1)
                dve.wait_ge(dv, n0 + len(taps))
                if not shared:
                    dve.tensor_tensor(ch(xb, c), acc[0], tb[:], ALU.add).then_inc(conv_done, 1)
                    return
                back = TAPS - PE_TAPS
                dve.wait_ge(pe_taps_done, c - KC + 3)
                dve.tensor_tensor(ch(xb, c), acc[0], tb[:], ALU.add).then_inc(dv, 1)
                dve.wait_ge(dv, n0 + len(taps) + 1)
                dve.tensor_tensor(ch(xb, c, back, T - back), ch(xb, c, back, T - back),
                                  ps[:, 1 + 2 * (c - KC + 2), back:T], ALU.add).then_inc(conv_done, 1)
                steps[0] += len(taps) + 1

            for c in range(4):
                glu(c, 2 * c)
            dve.wait_ge(tb_clear, 1)
            for c in range(3):
                conv(c, c % 2, steps[0])
                steps[0] += CHAIN
                if c < 2:
                    glu(4 + c, 2 * c)
            with loop(ET.DVE, 0, 3) as i:
                for s in range(2):
                    conv(2 * i + (3 + s), 1 - s, 2 * CHAIN * i + (steps[0] + CHAIN * s))
                    glu(2 * i + (6 + s), 2 * s)
            steps[0] += 6 * CHAIN
            conv(9, 1, steps[0])
            steps[0] += CHAIN
            with loop(ET.DVE, 0, 2) as i:
                for s in range(2):
                    conv(2 * i + (10 + s), s, 2 * CHAIN * i + (steps[0] + CHAIN * s))
                    glu(2 * i + (12 + s), 2 * s)
            steps[0] += 4 * CHAIN
            for c in (KC - 2, KC - 1):
                conv(c, c % 2, steps[0])

            a = 2 * KC + ADA_A1 - 1
            dve.wait_ge(ada_used, a)
            ada_reduce(a)
            ada_reduce(a + 1)
            a += 2
            dve.wait_ge(ln_used, KC - LATE)
            chain(dve.tensor_scalar(st[:, 12:16], ps[:, 0, 0:4], 1.0 / D, None, ALU.mult))
            chain(dve.tensor_tensor(st[:, 0:4], st[:, 12:16], st[:, 12:16], ALU.mult))
            chain(dve.scalar_tensor_tensor(st[:, 0:4], ps[:, 0, 4:8], 1.0 / D, st[:, 0:4], ALU.mult, ALU.subtract))
            chain(dve.tensor_scalar(st[:, 0:4], st[:, 0:4], 0.0, EPS, ALU.max, ALU.add))
            dve.reciprocal(st[:, 4:8], st[:, 0:4]).then_inc(var_done, 1)

            def z(k):
                if k < KC:
                    if k >= 2:
                        dve.wait_ge(hf_ready, KC + k - 1)
                    dve.tensor_tensor(scaled[k % 2][:], ch(xb, k), mu[:], ALU.subtract).then_inc(dv, 1)
                    steps[0] += 1
                if k >= 2:
                    lo_part(k - 2, KC + k - 2, silus[k % 2])
                if k < KC:
                    dve.wait_ge(dv, steps[0])
                    dve.tensor_tensor(normed[k % 2][:], scaled[k % 2][:], rstd[:], ALU.mult).then_inc(hf_ready, 1)

            def split_lo(q, off=0):
                dve.wait_ge(whi_done, q + 1 + off)
                dve.tensor_tensor(wlo[:, q % WS, :], raw[:, q % RAW, :], f(whi[:, q % WS, :]), ALU.subtract
                                  ).then_inc(wlo_done, 1)

            dve.wait_ge(rstd_done, 3)

            def gate1():
                dve.wait_ge(ada_used, M_SC2)
                dve.tensor_tensor(modb[:, M_G1:M_G1 + KC], mod[:, M_G1:M_G1 + KC], col("ada_b", M_G1, KC), ALU.add
                                  ).then_inc(small, 1)
                dve.wait_ge(small, n_small + 1)
                dve.tensor_tensor(g1b[:], modb[:, M_G1:M_G1 + KC], col("b_out", 0, KC), ALU.mult
                                  ).then_inc(small, 1)
                assert n_small + 2 == SMALL_G1

            for k in range(KC + 2):
                z(k)
                if k % 2 and k > 3:
                    ada_reduce(a)
                    a += 1
                    if a == M_SC2:
                        gate1()
            while a < 2 * KC + ADA_A1 + ADA_B0:
                ada_reduce(a)
                a += 1

            def x1(n):
                dve.wait_ge(yg_done, n + 1)
                dve.wait_ge(xr_in[n // 4], 16)
                dve.tensor_tensor(ch(xb, n), sig[:], ch(xb, n), ALU.add).then_inc(x1_done, 1)

            x1(0)
            x1(1)
            for n in range(2, 8):
                x1(n)
                add_squares(n - 2, ss1_done, x1sq_done)
            add_squares(6, ss1_done, x1sq_done)
            for j in range(8):
                for _ in range(ada_share(ADA_B1, j) - (j == 7)):
                    ada_reduce(a)
                    a += 1
                x1(8 + j)
                add_squares(7 + j, ss1_done, x1sq_done)
            add_squares(15, ss1_done, x1sq_done)
            ada_reduce(a)
            a += 1
            assert a == M_SH2 + SH2_EARLY
            dve.wait_ge(ada_used, a)
            dve.scalar_tensor_tensor(modb[:, M_SC2:M_SC2 + KC], mod[:, M_SC2:M_SC2 + KC], 1.0, b1p[:, KC:2 * KC],
                                     ALU.mult, ALU.add).then_inc(small, 1)
            dve.tensor_tensor(modb[:, M_SH2:a], mod[:, M_SH2:a], col("ada_b", M_SH2, SH2_EARLY), ALU.add
                              ).then_inc(small, 1)
            dve.wait_ge(small, SMALL_G1 + 2)
            dve.tensor_tensor(modb[:, M_SC2:M_SC2 + KC], modb[:, M_SC2:M_SC2 + KC], col("norm2_g", 0, KC), ALU.mult
                              ).then_inc(small, 1)
            dve.wait_ge(small, SMALL_G1 + 3)
            dve.wait_ge(stat_done, 2)
            variance(2)

            def h2(k):
                if k < KC:
                    if k >= 2:
                        dve.wait_ge(hf_ready, 2 * KC + k - 1)
                    dve.tensor_tensor(scaled[k % 2][:], ch(xb, k), rstd[:], ALU.mult).then_inc(dv, 1)
                    steps[0] += 1
                if k >= 2:
                    lo_part(k - 2, 2 * KC + k - 2, normed[k % 2])
                if k < KC:
                    dve.wait_ge(dv, steps[0])
                    if k >= 2:
                        dve.wait_ge(hlo_done, 2 * KC + k - 1)
                    dve.tensor_scalar(normed[k % 2][:], scaled[k % 2][:], modb[:, M_SC2 + k:M_SC2 + k + 1],
                                      modb[:, M_SH2 + k:M_SH2 + k + 1], ALU.mult, ALU.add).then_inc(hf_ready, 1)

            dve.wait_ge(rstd_done, 4)
            for k in range(KC + 2):
                h2(k)
                if (k in (5, 7) or k > 8) and a < ADA:
                    ada_reduce(a)
                    a += 1
                    if a == M_G2:
                        assert k < SH2_EARLY
                        late = slice(M_SH2 + SH2_EARLY, M_G2)
                        dve.wait_ge(ada_used, M_G2)
                        dve.tensor_tensor(modb[:, late], mod[:, late], col("ada_b", late.start, KC - SH2_EARLY),
                                          ALU.add).then_inc(small, 1)
                        dve.wait_ge(small, SMALL_G1 + 4)
            while a < ADA:
                ada_reduce(a)
                a += 1
            dve.wait_ge(ada_used, ADA)
            dve.tensor_tensor(modb[:, M_G2:M_G2 + KC], mod[:, M_G2:M_G2 + KC], col("ada_b", M_G2, KC), ALU.add
                              ).then_inc(x2_done, 1)

            def hidden_lo(j, off=0):
                dve.wait_ge(dhi_done, j + 1 + off)
                dve.tensor_tensor(ch(dlo, j % BLK), squares[j % 2][:], f(ch(dhi, j % BLK)), ALU.subtract).then_inc(dlo_done, 1)

            def x2(m, off=0):
                for nn in range(2):
                    n = 2 * m + nn
                    dve.scalar_tensor_tensor(ch(xb, n), ps[:, 4 + 2 * (m % 2) + nn, :],
                                             modb[:, M_G2 + n:M_G2 + n + 1], ch(xb, n), ALU.mult, ALU.add
                                             ).then_inc(x2_done, 1)

            for n in range(BLK + 1):
                if n < BLK:
                    r = first_squares[n % 4]
                    dve.wait_ge(relu_done, n + 1)
                    dve.tensor_tensor(r[:], r[:], r[:], ALU.mult).then_inc(dsq_done, 1)
                if n:
                    dve.wait_ge(dhi_done, n)
                    j = HIDDEN_ORDER[n - 1]
                    dve.tensor_tensor(ch(dlo, j), first_squares[(n - 1) % 4][:], f(ch(dhi, j)), ALU.subtract
                                      ).then_inc(dlo_done, 1)
            dve.wait_ge(wlo_done, LO_POOL)
            with loop(ET.DVE, 0, NBLK - 1) as b:
                for m in range(BLK):
                    dve.wait_ge(unit_done, 16 * b + (W2_0 + m + 1))
                    if m == 0:
                        dve.wait_ge(x2_done, 16 * b + 1)
                    x2(m)
                    split_lo(W2_0 + m + 2, 16 * b)
                for j in range(BLK):
                    hidden_lo(BLK + j, 8 * b)
                    split_lo(W2_0 + BLK + j + 2, 16 * b)
            q = W2_0 + 16 * (NBLK - 1)
            for m in range(BLK):
                dve.wait_ge(unit_done, q + m + 1)
                if m == 0:
                    dve.wait_ge(x2_done, 16 * (NBLK - 1) + 1)
                x2(m)
                if m < BLK - 2:
                    split_lo(q + m + 2)
                add_squares(2 * m, ss2_done, x2sq_done, sq)
                add_squares(2 * m + 1, ss2_done, x2sq_done, ta)
            dve.wait_ge(stat_done, 3)
            variance(0)
            dve.wait_ge(fg_done, KC)
            dve.wait_ge(rstd_done, 5)
            for n in range(FIN_POOL):
                dve.tensor_tensor(ch(xb, n), ch(xb, n), ps[:, 1, :], ALU.mult).then_inc(fin_dve, 1)

        @block.gpsimd
        def _(pool):
            def split_lo(q, off=0):
                pool.wait_ge(whi_done, q + 1 + off)
                pool.tensor_tensor(wlo[:, q % WS, :], raw[:, q % RAW, :], f(whi[:, q % WS, :]), ALU.subtract
                                   ).then_inc(wlo_done, 1)

            def c_sums(c):
                pool.wait_ge(conv_done, c + 2)
                pool.wait_ge(s1_done, c + 1)
                pool.tensor_tensor(s1[:], s1[:], ch(xb, c), ALU.add).then_inc(s1_done, 1)
                pool.wait_ge(csq_done, c + 1)
                pool.wait_ge(s2_done, c + 1)
                pool.tensor_tensor(s2[:], s2[:], sq[:], ALU.add).then_inc(s2_done, 1)

            pool.memset(ident[:], 0.0).then_inc(ident_clear, 1)
            pool.wait_ge(ident_clear, 1)
            pool.affine_select(out=ident[:], in_=ident[:], compare_op=ALU.not_equal, fill=1.0, base=0,
                               pattern=[[-1, P]], channel_multiplier=1).then_inc(ident_set, 1)
            pool.memset(s1[:], 0.0).then_inc(s1_done, 1)
            pool.memset(s2[:], 0.0).then_inc(s2_done, 1)
            for q in range(A0, A1 + 2):
                split_lo(q)
            pool.wait_ge(ada_used, 2 * KC)
            pool.wait_ge(cs_ready, 1)
            def side_sums(c):
                pool.wait_ge(side_mul, c + 1)
                for n, (src, j) in enumerate(zip((ta, ssum, rstd), SIDE[1:])):
                    part = slice(TAPS - 1 - j, T)
                    if n:
                        pool.wait_ge(side_add, 3 * c + n)
                    pool.tensor_tensor(pacc[:, part], pacc[:, part], src[:, part], ALU.add).then_inc(side_add, 1)

            def ada_product(a, off=0):
                wait_ada(pool, a, off)
                pool.tensor_tensor(adar[:, a % 2, :], adar[:, a % 2, :], csb[:], ALU.mult).then_inc(ada_mul, 1)

            def a1_chunk(i, s):
                split_lo(A1 + 2 + 2 * s, 4 * i)
                if not (isinstance(i, int) and i == 0 and s == 0):
                    c_sums(2 * i + (s - 1))
                split_lo(A1 + 3 + 2 * s, 4 * i)
                side_sums(2 * i + (2 + s))
                ada_product(2 * KC + s, 2 * i)

            side_sums(0)
            side_sums(1)
            a1_chunk(0, 0)
            a1_chunk(0, 1)
            with loop(ET.Pool, 1, 4) as i:
                a1_chunk(i, 0)
                a1_chunk(i, 1)
            for c in range(12, KC):
                q = A1 + 2 * (c - 4)
                split_lo(q + 2)
                c_sums(c - 5)
                if c == 12:
                    side_sums(10)
                if c == KC - 1:
                    side_sums(14)
                split_lo(q + 3)
                side_sums(c - 1 if c < KC - 1 else c)
                if c < KC - 1:
                    ada_product(2 * KC + c - 4)
            c_sums(11)
            c_sums(12)
            c_sums(13)
            for q in range(B0 + 2, LO_POOL):
                split_lo(q)
            pool.wait_ge(fg_done, KC)
            pool.wait_ge(rstd_done, 5)
            for n in range(FIN_POOL, KC):
                pool.tensor_tensor(ch(xb, n), ch(xb, n), rstd[:], ALU.mult).then_inc(fin_pool, 1)


def _tiles(m, rows, cols):
    t = m.reshape(m.shape[0] // P, P, m.shape[1] // P, P)[rows][:, :, cols]
    return t.transpose(1, 0, 2, 3).reshape(P, -1)


def _units(w_in, w_out, w1, w2):
    every = list(range(KC))
    in_cols = [h * KC + c for c in range(4) for h in range(2)]
    for j in range(8):
        yield _tiles(w_in, [2 * j, 2 * j + 1], in_cols)
    for c in range(4, KC):
        for h in range(2):
            yield _tiles(w_in, every, [h * KC + c])
    for j in range(8):
        yield _tiles(w_out, [2 * j, 2 * j + 1], list(range(8)))
    for j in range(8):
        yield _tiles(w_out, every, [8 + j])
    for b in range(NBLK):
        for j in range(BLK):
            if b == 0:
                yield _tiles(w1, [2 * j, 2 * j + 1], list(range(8)))
            else:
                yield _tiles(w1, every, [BLK * b + j])
        rows = list(range(BLK * b, BLK * (b + 1)))
        for m in range(BLK):
            yield np.concatenate([_tiles(w2, rows, [2 * m + nn]) for nn in range(2)], axis=1)


def kernel(x, c, ada_w, ada_b, norm1_g, norm2_g, mlp_w1, mlp_w2, final_g, conv_w_in, conv_b_in, conv_w_dw,
           conv_b_dw, conv_ln_g, conv_ln_b, conv_w_out, conv_b_out, **other_mixers):
    import concourse.bacc as bacc
    from concourse.bass_utils import run_bass_kernel_spmd

    def chunks(v):
        return np.asarray(v).reshape(-1, P).T

    order = [h * KC + k for k in range(KC) for h in (1, 0)]
    order += [part * KC + k for part in (2, 4, 3, 5) for k in range(KC)]
    w = np.stack(list(_units(np.asarray(conv_w_in)[0], np.asarray(conv_w_out)[0],
                             np.asarray(mlp_w1)[0], np.asarray(mlp_w2)[0])))
    ada = np.ascontiguousarray(np.asarray(ada_w)[0].T.reshape(ADA, P, D)[order])
    dw = np.asarray(conv_w_dw)[0].T.reshape(KC, P, TAPS).transpose(1, 0, 2).reshape(P, -1)
    packed = {"ada_b": chunks(np.asarray(ada_b)[0])[:, order], "norm1_g": chunks(norm1_g), "norm2_g": chunks(norm2_g),
              "final_g": chunks(final_g), "b_in": chunks(conv_b_in), "b_dw": chunks(conv_b_dw),
              "ln_g": chunks(conv_ln_g), "ln_b": chunks(conv_ln_b), "b_out": chunks(conv_b_out), "w_dw": dw}
    arrays = {
        "xT": np.ascontiguousarray(np.asarray(x)[0].T),
        "c": np.ascontiguousarray(np.asarray(c)[0]),
        "w": w,
        "ada": ada,
        "par": np.ascontiguousarray(np.concatenate([packed[name] for name, _ in PARAMS], axis=1)),
    }
    nc = bacc.Bacc("TRN2", target_bir_lowering=False, num_devices=1)
    aps = {n: nc.dram_tensor(n, a.shape, F32, kind="ExternalInput").ap() for n, a in arrays.items()}
    out = nc.dram_tensor("out", (D, T), F32, kind="ExternalOutput").ap()
    trunk_kernel(nc, aps["xT"], aps["c"], aps["w"].rearrange("q p n -> p q n"),
                 aps["ada"].rearrange("a p n -> p a n"), aps["par"], out)
    r = run_bass_kernel_spmd(nc, [arrays], core_ids=[0])
    return np.ascontiguousarray(r.results[0]["out"].T).reshape(1, T, D)
```
